# Optimizing a Trainium2 kernel written in Bass

```python
import jax, jax.numpy as jnp
from jax import lax
import numpy as np

D_MODEL = 1024
BATCH = 1
SEQ = 1024
DEPTH = 1

D_MIX = D_MODEL
RET_HEADS = 4
RET_QK_DIM = 64
RET_V_DIM = 128
RET_QK = RET_HEADS * RET_QK_DIM
RET_WIDTH = RET_HEADS * RET_V_DIM
GDN_HEADS = 4
GDN_HEAD_DIM = 128
GDN_WIDTH = GDN_HEADS * GDN_HEAD_DIM
CONV_K = 4
CONV_CH = 3 * GDN_WIDTH
CHUNK = 128
ROPE_BASE = 10000.0
NORM_EPS = 1e-6
PEER_HEADS = 8
PEER_KEYS = 128
PEER_EXPERTS = PEER_KEYS * PEER_KEYS
PEER_QDIM = 256
PEER_HALF = PEER_QDIM // 2
PEER_TOPK = 16
PEER_BLOCK = 128
SPLITS = (RET_QK, RET_QK, RET_WIDTH, RET_WIDTH, GDN_WIDTH, GDN_WIDTH, GDN_WIDTH, GDN_WIDTH, GDN_HEADS, GDN_HEADS)
IN_COLS = sum(SPLITS)

kernel_name = 'hybrid_retention_gdn_peer'

def _rmsnorm(x, w):
    xf = x.astype(jnp.float32)
    y = xf * lax.rsqrt(jnp.mean(xf * xf, axis=-1, keepdims=True) + NORM_EPS)
    return (y * w.astype(jnp.float32)).astype(x.dtype)

def _heads(t, n_heads):
    b, t_len, _ = t.shape
    return t.reshape(b, t_len, n_heads, -1).transpose(0, 2, 1, 3)

def _rope(t):
    t_len, d = t.shape[-2], t.shape[-1]
    half = d // 2
    inv = ROPE_BASE ** (-jnp.arange(half, dtype=jnp.float32) / half)
    ang = jnp.arange(t_len, dtype=jnp.float32)[:, None] * inv[None, :]
    cos, sin = jnp.cos(ang), jnp.sin(ang)
    t1, t2 = t[..., :half], t[..., half:]
    return jnp.concatenate([t1 * cos - t2 * sin, t1 * sin + t2 * cos], axis=-1)

def _retention(q, k, v):
    b, h, t_len, dk = q.shape
    n = t_len // CHUNK
    lg = jnp.log1p(-jnp.exp2(-5.0 - jnp.arange(h, dtype=jnp.float32)))
    k = k * (dk ** -0.5)
    q = q.reshape(b, h, n, CHUNK, dk)
    k = k.reshape(b, h, n, CHUNK, dk)
    v = v.reshape(b, h, n, CHUNK, -1)
    idx = jnp.arange(CHUNK, dtype=jnp.float32)
    diff = idx[:, None] - idx[None, :]
    decay = jnp.where(diff >= 0, jnp.exp(lg[:, None, None] * jnp.maximum(diff, 0.0)), 0.0)
    scores = jnp.einsum('bhnid,bhnjd->bhnij', q, k) * decay[None, :, None]
    intra = jnp.einsum('bhnij,bhnje->bhnie', scores, v)
    k_dec = k * jnp.exp(lg[:, None] * (CHUNK - 1.0 - idx))[None, :, None, :, None]
    chunk_kv = jnp.einsum('bhncd,bhnce->nbhde', k_dec, v)
    chunk_decay = jnp.exp(lg * CHUNK)[None, :, None, None]

    def step(state, kv):
        return state * chunk_decay + kv, state

    _, s_prev = lax.scan(step, jnp.zeros_like(chunk_kv[0]), chunk_kv)
    q_dec = q * jnp.exp(lg[:, None] * (idx + 1.0))[None, :, None, :, None]
    inter = jnp.einsum('bhncd,nbhde->bhnce', q_dec, s_prev)
    return (intra + inter).reshape(b, h, t_len, -1)

def _gated_delta_rule(q, k, v, g, beta):
    b, h, t_len, dk = q.shape
    dv = v.shape[-1]
    n = t_len // CHUNK
    q = (q * (dk ** -0.5)).reshape(b, h, n, CHUNK, dk)
    k = k.reshape(b, h, n, CHUNK, dk)
    v = v.reshape(b, h, n, CHUNK, dv)
    g = g.reshape(b, h, n, CHUNK)
    beta = beta.reshape(b, h, n, CHUNK)
    gc = jnp.cumsum(g, axis=-1)
    causal = jnp.tril(jnp.ones((CHUNK, CHUNK), dtype=bool))
    strict = jnp.tril(jnp.ones((CHUNK, CHUNK), dtype=bool), -1)
    gdiff = gc[..., :, None] - gc[..., None, :]
    lmask = jnp.where(causal, jnp.exp(jnp.where(causal, gdiff, 0.0)), 0.0)
    kb = k * beta[..., None]
    kkt = jnp.einsum('bhnid,bhnjd->bhnij', kb, k) * lmask
    m = jnp.eye(CHUNK, dtype=kkt.dtype) + jnp.where(strict, kkt, 0.0)
    rhs = jnp.concatenate([v * beta[..., None], kb * jnp.exp(gc)[..., None]], axis=-1)
    sol = lax.linalg.triangular_solve(m, rhs, left_side=True, lower=True, unit_diagonal=True)
    u, w = sol[..., :dv], sol[..., dv:]
    attn = jnp.einsum('bhnid,bhnjd->bhnij', q, k) * lmask
    q_dec = q * jnp.exp(gc)[..., None]
    glast = gc[..., -1:]
    k_st = k * jnp.exp(glast - gc)[..., None]
    dec = jnp.exp(glast[..., 0])
    xs = tuple(jnp.moveaxis(t, 2, 0) for t in (q_dec, attn, u, w, k_st, dec))

    def step(state, inp):
        qd, at, uc, wc, ks, dc = inp
        v_new = uc - jnp.einsum('bhcd,bhde->bhce', wc, state)
        o = jnp.einsum('bhcd,bhde->bhce', qd, state) + jnp.einsum('bhij,bhje->bhie', at, v_new)
        state = state * dc[..., None, None] + jnp.einsum('bhcd,bhce->bhde', ks, v_new)
        return state, o

    s0 = jnp.zeros((b, h, dk, dv), dtype=q.dtype)
    _, o = lax.scan(step, s0, xs)
    return jnp.moveaxis(o, 0, 2).reshape(b, h, t_len, dv)

def _causal_short_conv(x, w):
    ch = x.shape[-1]
    return lax.conv_general_dilated(x, w[:, None, :], window_strides=(1,), padding=[(CONV_K - 1, 0)],
                                    dimension_numbers=('NWC', 'WIO', 'NWC'), feature_group_count=ch)

def _peer(h, wq, sub_keys, u_tab, v_tab):
    b, t_len, d = h.shape
    hb = h.reshape(-1, PEER_BLOCK, d)

    def block(xb):
        q = (xb @ wq).reshape(PEER_BLOCK, PEER_HEADS, 2, PEER_HALF)
        s = jnp.einsum('thpd,hpkd->thpk', q, sub_keys).astype(jnp.float32)
        s1, i1 = lax.top_k(s[:, :, 0], PEER_TOPK)
        s2, i2 = lax.top_k(s[:, :, 1], PEER_TOPK)
        cand = (s1[..., :, None] + s2[..., None, :]).reshape(PEER_BLOCK, PEER_HEADS, -1)
        cid = (i1[..., :, None] * PEER_KEYS + i2[..., None, :]).reshape(PEER_BLOCK, PEER_HEADS, -1)
        best, pos = lax.top_k(cand, PEER_TOPK)
        ids = jnp.take_along_axis(cid, pos, axis=-1).reshape(PEER_BLOCK, -1)
        gate = jax.nn.softmax(best, axis=-1).reshape(PEER_BLOCK, -1)
        act = jax.nn.gelu(jnp.einsum('tkd,td->tk', u_tab[ids], xb).astype(jnp.float32), approximate=False)
        return jnp.einsum('tk,tkd->td', (gate * act).astype(xb.dtype), v_tab[ids])

    return lax.map(block, hb).reshape(b, t_len, d)

def setup_inputs(seed: int = 0) -> dict:
    key = jax.random.key(seed)
    ks = jax.random.split(key, 16)
    f32 = jnp.float32

    def nrm(k, shape, scale):
        return jax.random.normal(k, shape, f32) * scale

    x = nrm(ks[0], (BATCH, SEQ, D_MODEL), 1.0)
    ln1_w = 1.0 + nrm(ks[1], (DEPTH, D_MODEL), 0.02)
    w_in = nrm(ks[2], (DEPTH, D_MODEL, IN_COLS), D_MODEL ** -0.5)
    ret_norm_w = 1.0 + nrm(ks[3], (DEPTH, RET_WIDTH), 0.02)
    conv_w = nrm(ks[4], (DEPTH, CONV_K, CONV_CH), CONV_K ** -0.5)
    A_log = jnp.log(jax.random.uniform(ks[5], (DEPTH, GDN_HEADS), f32, 1.0, 16.0))
    dt = jnp.exp(jax.random.uniform(ks[6], (DEPTH, GDN_HEADS), f32, np.log(1e-3), np.log(1e-1)))
    dt_bias = dt + jnp.log(-jnp.expm1(-dt))
    gdn_norm_w = 1.0 + nrm(ks[7], (DEPTH, GDN_HEAD_DIM), 0.02)
    w_out = nrm(ks[8], (DEPTH, D_MIX, D_MODEL), D_MIX ** -0.5)
    ln2_w = 1.0 + nrm(ks[9], (DEPTH, D_MODEL), 0.02)
    peer_wq = nrm(ks[10], (DEPTH, D_MODEL, PEER_HEADS * PEER_QDIM), D_MODEL ** -0.5)
    peer_keys = nrm(ks[11], (DEPTH, PEER_HEADS, 2, PEER_KEYS, PEER_HALF), PEER_HALF ** -0.5)
    peer_u = nrm(ks[12], (DEPTH, PEER_EXPERTS, D_MODEL), D_MODEL ** -0.5)
    peer_v = nrm(ks[13], (DEPTH, PEER_EXPERTS, D_MODEL), PEER_HEADS ** -0.5)
    lnf_w = 1.0 + nrm(ks[14], (D_MODEL,), 0.02)
    return {'x': x, 'ln1_w': ln1_w, 'w_in': w_in, 'ret_norm_w': ret_norm_w, 'conv_w': conv_w,
            'A_log': A_log, 'dt_bias': dt_bias, 'gdn_norm_w': gdn_norm_w, 'w_out': w_out,
            'ln2_w': ln2_w, 'peer_wq': peer_wq, 'peer_keys': peer_keys, 'peer_u': peer_u,
            'peer_v': peer_v, 'lnf_w': lnf_w}

def reference(x, ln1_w, w_in, ret_norm_w, conv_w, A_log, dt_bias, gdn_norm_w, w_out,
              ln2_w, peer_wq, peer_keys, peer_u, peer_v, lnf_w):
    f32 = jnp.float32
    offsets = [int(o) for o in np.cumsum(SPLITS)[:-1]]
    for l in range(DEPTH):
        h = _rmsnorm(x, ln1_w[l])
        proj = (h @ w_in[l]).astype(f32)
        rq, rk, rv, rg, gq, gk, gv, gz, ga, gb = jnp.split(proj, offsets, axis=-1)

        q_r = _rope(_heads(rq, RET_HEADS))
        k_r = _rope(_heads(rk, RET_HEADS))
        o_r = _retention(q_r, k_r, _heads(rv, RET_HEADS))
        mu = jnp.mean(o_r, axis=-1, keepdims=True)
        var = jnp.mean(jnp.square(o_r - mu), axis=-1, keepdims=True)
        o_r = ((o_r - mu) * lax.rsqrt(var + NORM_EPS)).transpose(0, 2, 1, 3).reshape(x.shape[0], x.shape[1], RET_WIDTH)
        y_r = o_r * ret_norm_w[l].astype(f32) * jax.nn.silu(rg)

        qkv = jax.nn.silu(_causal_short_conv(jnp.concatenate([gq, gk, gv], axis=-1), conv_w[l].astype(f32)))
        cq, ck, cv = jnp.split(qkv, 3, axis=-1)
        q_g = _heads(cq, GDN_HEADS)
        k_g = _heads(ck, GDN_HEADS)
        q_g = q_g * lax.rsqrt(jnp.sum(q_g * q_g, axis=-1, keepdims=True) + NORM_EPS)
        k_g = k_g * lax.rsqrt(jnp.sum(k_g * k_g, axis=-1, keepdims=True) + NORM_EPS)
        g_dec = -jnp.exp(A_log[l].astype(f32)) * jax.nn.softplus(ga + dt_bias[l].astype(f32))
        beta = jax.nn.sigmoid(gb)
        o_g = _gated_delta_rule(q_g, k_g, _heads(cv, GDN_HEADS),
                                g_dec.transpose(0, 2, 1), beta.transpose(0, 2, 1))
        o_g = _rmsnorm(o_g.transpose(0, 2, 1, 3), gdn_norm_w[l].astype(f32))
        y_g = o_g.reshape(x.shape[0], x.shape[1], GDN_WIDTH) * jax.nn.silu(gz)

        mixed = jnp.concatenate([y_r, y_g], axis=-1).astype(x.dtype)
        x = x + mixed @ w_out[l]

        h2 = _rmsnorm(x, ln2_w[l])
        x = x + _peer(h2, peer_wq[l], peer_keys[l], peer_u[l], peer_v[l])
    return _rmsnorm(x, lnf_w)


_drawn_inputs = setup_inputs


def setup_inputs(seed=0):
    import zlib

    import numpy as np

    out = dict(_drawn_inputs(seed))
    spreads = {}
    factors = {'ret_norm_w': 43.566, 'gdn_norm_w': 40.732, 'lnf_w': 23.71, 'ln2_w': 17.854}
    for name, (base, spread) in spreads.items():
        noise = np.random.default_rng([zlib.crc32(name.encode()), seed]).standard_normal(out[name].shape)
        drawn = base * np.exp(spread * noise) if base else spread * noise
        out[name] = __import__('jax').numpy.asarray(drawn.astype(out[name].dtype))
    for name, factor in factors.items():
        out[name] = (out[name] * factor).astype(out[name].dtype)
    return out
```

```python
from contextlib import ExitStack

import concourse.bass as bass
import numpy as np
from concourse import mybir

ALU = mybir.AluOpType
ACT = mybir.ActivationFunctionType
AX = mybir.AxisListType.X
F32 = mybir.dt.float32
U32 = mybir.dt.uint32

P = 128
D = 1024
KT = D // P
SEQ = 1024
NCH = SEQ // P
H = 4
DV = 128
EPS = 1e-6
WB = 256
IN_BLOCKS, OUT_BLOCKS, Q_BLOCKS = 14, 4, 8
BLOCKS = IN_BLOCKS + OUT_BLOCKS + Q_BLOCKS
PH, TOPK, KEYS = 8, 16, 128
SLOTS = PH * TOPK
QUARTER = 4
TURNS = SLOTS // QUARTER
LAG = 6
RING = 8
LEVELS = 7
LOWEST = -3.0e38
COUNT0 = 64
LATE = 2
TAB = 1 + 1 + 1 + 1 + LEVELS + H

USES = (
    [("hT", 2, 0), ("hT", 2, 1), ("qk_in", 1, 0), ("vr_in", 1, 0), ("gR_in", 1, 0), ("conv_in", 3, 0),
     ("conv_in", 3, 1), ("conv_in", 3, 2), ("gG_in", 1, 0), ("ab_in", 1, 0), ("retT", 1, 0), ("ret_s", 1, 0),
     ("ret_norm", 1, 0), ("ret_state", 1, 0), ("gc_in", 1, 0), ("E", 1, 0), ("kbT", 1, 0),
     ("norm_in", 2, 0), ("norm_in", 2, 1), ("kst", 1, 0), ("vb", 1, 0), ("NT", 1, 0), ("attn", 1, 0)]
    + [(e, LEVELS, i) for i in range(LEVELS) for e in ("inv_P", "inv_T", "inv_TT")]
    + [("wT", 1, 0), ("vnew", 1, 0), ("gdn_norm", 1, 0), ("gdn_state", 1, 0), ("mT", 2, 0), ("mT", 2, 1),
       ("x2", 2, 0), ("x2", 2, 1), ("h2T", 2, 0), ("h2T", 2, 1)]
    + [("qT", 4, i) for i in range(4)] + [("scores", 4, i) for i in range(4)]
)
BANKS = 6
NUSE = -(-len(USES) // BANKS) * BANKS


def build(nc, x, w, w_ab, keysT, u_tab, v_tab, cols, rows, head_rows, tables, rope, qdec, small, out):
    with ExitStack() as ctx:
        def sb(name, shape, dt=F32):
            return ctx.enter_context(nc.sbuf_tensor(name, [P, *shape], dt))

        def sem(name):
            return ctx.enter_context(nc.semaphore(name))

        tab = sb("tab", [TAB, P])
        ident, causal, strict, ones = (tab[:, i, :] for i in range(4))
        level_mask = [tab[:, 4 + i, :] for i in range(LEVELS)]
        ret_decay = tab[:, 4 + LEVELS:4 + LEVELS + H, :]
        ropes = sb("ropes", [3, NCH, 32])
        ret_qdec = sb("ret_qdec", [H, P])
        smalls = sb("smalls", [10])
        lnT = sb("lnT", [KT])
        conv_w = sb("conv_w", [12, 4])
        rowsb = sb("rowsb", [2, D])
        ln2_row, lnf_row = rowsb[:, 0, :], rowsb[:, 1, :]
        headsb = sb("headsb", [5 * P + 2 * H])
        retw_row, gdnw_row = headsb[:, 0:512], headsb[:, 512:640]
        a_log, dt_bias = headsb[:, 640:644], headsb[:, 644:648]
        neg_a = sb("neg_a", [H])
        eps_col = sb("eps_col", [1])
        w_ab_sb = sb("w_ab_sb", [KT, 2 * H])
        keys_sb = sb("keys_sb", [16, P])

        wbuf = [sb(f"wbuf{i}", [KT, WB]) for i in range(2)]
        x_in = sb("x_in", [D])
        x2 = sb("x2_row", [D])
        rowbuf = sb("rowbuf", [D])
        actT = sb("actT", [KT, P])
        qk_r = sb("qk_r", [2 * H, 2, 32])
        v_r = sb("v_r", [H, DV])
        gate_r = sb("gate_r", [H, DV])
        gate_g = sb("gate_g", [H, DV])
        ab = sb("ab", [2, H])
        conv_in = sb("conv_in", [12, P + 3])
        area = sb("area", [10, 256])
        ret_rot = area[:, 0:2, :].rearrange("p a (h z d) -> p (a h) z d", z=2, d=32)
        ret_tmp = area[:, 2:4, :].rearrange("p a (h z d) -> p (a h) z d", z=2, d=32)
        retT = area[:, 4:6, :].rearrange("p a (b t) -> p (a b) t", t=P)
        ret_qz = area[:, 2:4, :].rearrange("p a (b t) -> p (a b) t", t=P)
        ret_qd = area[:, 0:2, :].rearrange("p a (b t) -> p (a b) t", t=P)
        ret_kd = area[:, 7, :].rearrange("p (h d) -> p h d", d=64)
        ret_s = area[:, 8:10, :].rearrange("p a (b t) -> p (a b) t", t=P)
        flat = area[:, :, :].rearrange("p a b -> p (a b)")
        conv = flat[:, 0:1536].rearrange("p (c t) -> p c t", t=P)
        norms = flat[:, 1536:2560].rearrange("p (c t) -> p c t", t=P)
        cmask = sb("decayT", [H, P])
        expg = sb("expg", [H, P])
        vb = sb("vb", [H, DV])
        kst = sb("kst", [H, P])
        vnew = sb("vnew", [H, DV])
        qdT = sb("qdT", [H, P])
        state_g = sb("state_g", [H, DV])
        state_r = sb("state_r", [2, DV])
        arena = sb("arena", [16, 256])
        half = lambda i: arena[:, 2 * i:2 * i + 2, :].rearrange("p a (b t) -> p (a b) t", t=P)
        NT, attnT, T, TT, Pm, kbe, wT, kbT = (half(i) for i in range(8))
        qT = arena[:, 0:8, :].rearrange("p a (b t) -> p (a b) t", t=P)
        scores = arena[:, 8:16, :].rearrange("p a (b t) -> p (a b) t", t=P)
        cand = qT.rearrange("p (h z) t -> p h (z t)", z=2)
        picked = scores.rearrange("p a (b t) -> p (a b) t", t=TOPK)
        st = sb("st", [64])
        bn = sb("bn", [H, 6])
        mv = sb("mv", [H, 2])
        top_v = sb("top_v", [16, TOPK])
        top_i = sb("top_i", [16, TOPK], U32)
        top_if = sb("top_if", [16, TOPK])
        best = sb("best", [PH, TOPK])
        pos = sb("pos", [SLOTS], U32)
        pos2 = sb("pos2", [2, SLOTS], U32)
        pos_f = sb("pos_f", [2, SLOTS])
        sel = sb("sel", [2, SLOTS])
        gate_next = sb("gate_next", [SLOTS])
        ids_next = sb("ids_next", [SLOTS])
        iota_f = sb("iota_f", [TOPK])

        urow = [sb(f"urow{i}", [D]) for i in range(RING)]
        vrow = [sb(f"vrow{i}", [D]) for i in range(RING)]
        h2 = sb("h2", [D])
        ids = sb("ids", [SLOTS], U32)
        gate = sb("gate", [SLOTS])
        dots = sb("dots", [SLOTS])
        gelu = sb("gelu", [SLOTS])
        weight = sb("weight", [SLOTS])
        diag = sb("diag", [TOPK, P])
        y_sb = diag[:, 0:D // P, :].rearrange("p k t -> p (k t)")

        bank = [ctx.enter_context(nc.psum_tensor(f"bank{i}", [P, 512], F32)) for i in range(BANKS)]
        y_ps = [ctx.enter_context(nc.psum_tensor(f"y_ps{i}", [P, 512], F32)) for i in range(2)]

        per_chunk = {
            "rms1": 1, "sqrt1": 1, "x_norm": 1, "rot": 1, "ret_qd": 1, "ret_out_ready": 1, "sqrt_ret": 1,
            "ret_mixed": 1, "conv_done": 1, "silu_conv": 1, "sq": 1, "normed": 1, "sp_in": 1, "exp_ab": 1,
            "ln_ab": 1, "beta_g": 1, "diff": 1, "exp_diff": 1, "small_exp": 1, "kst_scale": 1, "qd": 1,
            "kbe": 1, "T_init": 1, "gdn_ss": 1, "gdn_ms": 1, "sqrt_gdn": 1, "mixed": 1, "rms2": 1,
            "sqrt2": 1, "h2": 1, "gate_in": 1, "gate_exp": 1, "routed": 1,
            "peer_in": 1, "ids_late": 1, "gelu": PH, "weight": PH, "diag": SLOTS, "yss": 1, "yms": 1,
            "sqrt_y": 1, "y_out": 1, "pe_done": 1,
        }
        for e, m, _ in USES:
            per_chunk[e] = m
        S = {e: sem(e) for e in per_chunk}
        full = sem("bank_full")
        const_in, x_loaded, y_stored = sem("const_in"), sem("x_loaded"), sem("y_stored")
        start_up = sem("start_up")
        passed = sem("passed")
        w_loaded = [sem(f"w_loaded{i}") for i in range(2)]
        w_free = sem("w_free")
        u_loaded = [sem(f"u_loaded{i}") for i in range(RING)]
        v_loaded = [sem(f"v_loaded{i}") for i in range(RING)]
        u_used, v_used = sem("u_used"), sem("v_used")
        mix_chain, peer_chain = sem("mix_chain"), sem("peer_chain")
        N_CONST = 11

        def event(name, n, i=0):
            return S[name], n * per_chunk[name] + i + 1

        def event_before(name, n):
            return S[name], n * per_chunk[name]

        def used(sem_, n, s):
            return sem_, n * SLOTS + (s + 1 + COUNT0)

        def follows(eng, name, n):
            if not isinstance(n, int) or n > 0:
                eng.wait_ge(*event_before(name, n))

        block = ctx.enter_context(nc.Block())

        @block.sync
        def _(sp):
            for dst, src in ((tab[:, :, :], tables), (ropes[:, :, :, :], rope), (ret_qdec[:, :, :], qdec),
                             (smalls[:, :], small), (lnT[:, :], cols[:, 0:KT]),
                             (conv_w[:, :, :], cols[:, KT:].rearrange("p (c j) -> p c j", j=4)),
                             (w_ab_sb[:, :, :], w_ab), (keys_sb[:, :, :], keysT),
                             (ln2_row, rows[0].partition_broadcast(P)), (lnf_row, rows[1].partition_broadcast(P)),
                             (headsb[:, :], head_rows.partition_broadcast(P))):
                sp.dma_start(dst, src).then_inc(const_in, 16)
            sp.dma_start(x_in[:, :], x[0]).then_inc(x_loaded, 16)

            def blocks(n):
                with sp.Fori(0, BLOCKS // 2) as b:
                    for i in range(2):
                        sp.wait_ge(w_free, n * BLOCKS + b * 2 + (i + 1))
                        sp.dma_start(wbuf[i][:, :, :], w[bass.ds(b * 2 + i, 1)].rearrange("o p k c -> (o p) k c")
                                     ).then_inc(w_loaded[i], 16)

            with sp.Fori(0, NCH - 1) as n:
                blocks(n)
                sp.wait_ge(*event("x2", n, 1))
                sp.dma_start(x_in[:, :], x[bass.ds(n + 1, 1)].rearrange("o p d -> (o p) d")).then_inc(x_loaded, 16)
            blocks(NCH - 1)

        @block.gpsimd
        def _(pool):
            nc.gpsimd.iota(pos[:, 0:TOPK], [[1, TOPK]], base=0, channel_multiplier=0).then_inc(start_up, 1)
            pool.wait_ge(start_up, 1)
            nc.gpsimd.tensor_copy(iota_f[:, :], pos[:, 0:TOPK]).then_inc(start_up, 1)

            def gather(table, row, slot, done):
                nc.gpsimd.indirect_dma_start(
                    out=row, out_offset=None, in_=table,
                    in_offset=bass.IndirectOffsetOnAxis(ap=ids[:, slot:slot + 1], axis=0)).then_inc(done, 16)

            with pool.Fori(0, NCH) as n:
                pool.wait_ge(*event("peer_in", n))
                pool.sem_inc(passed, 1)
                for t in range(TURNS + LAG):
                    for q in range(QUARTER):
                        s = QUARTER * t + q
                        if s == SLOTS - LATE * TOPK:
                            pool.wait_ge(*event("ids_late", n))
                            pool.sem_inc(passed, 1)
                        if s < SLOTS:
                            pool.wait_ge(*used(u_used, n, s - RING))
                            pool.sem_inc(passed, 1)
                            gather(u_tab, urow[s % RING][:, :], s, u_loaded[s % RING])
                        s -= QUARTER * LAG
                        if s >= 0:
                            pool.wait_ge(*used(v_used, n, s - RING))
                            pool.sem_inc(passed, 1)
                            gather(v_tab, vrow[s % RING][:, :], s, v_loaded[s % RING])

        @block.tensor
        def _(pe):
            pe.wait_ge(const_in, 16 * N_CONST)
            mm, tr = nc.tensor.matmul, nc.tensor.transpose

            def peer_turn(n, t):
                if t == LAG:
                    pe.wait_ge(*event("x2", n, 1))
                    pe.wait_ge(S["y_out"], n + 1)
                    for j in range(2):
                        mm(y_ps[j][:, :], ident, x2[:, 512 * j:512 * j + 512], start=True, stop=False,
                           skip_group_check=True)
                for s in range(QUARTER * (t - LAG), QUARTER * (t - LAG + 1)):
                    if s < 0 or s >= SLOTS:
                        continue
                    pe.wait_ge(*event("diag", n, s))
                    pe.wait_ge(v_loaded[s % RING], n * (16 * SLOTS // RING) + 16 * (s // RING + 1))
                    for j in range(2):
                        last = mm(y_ps[j][:, :], diag[:, s % TOPK, :], vrow[s % RING][:, 512 * j:512 * j + 512],
                                  start=False, stop=(s == SLOTS - 1), skip_group_check=True)
                    last.then_inc(v_used, 1)

            def mix(n, turn):
                use = [0]

                def take():
                    u = use[0]
                    use[0] += 1
                    v = u - BANKS
                    if v >= 0:
                        pe.wait_ge(*event(USES[v][0], n, USES[v][2]))
                    elif not isinstance(n, int) or n > 0:
                        v += NUSE
                        while v >= len(USES):
                            v -= BANKS
                        pe.wait_ge(*event(USES[v][0], n - 1, USES[v][2]))
                    return bank[u % BANKS]

                def given(ins):
                    ins.then_inc(full, 1)

                def transposes(src, count):
                    b = take()
                    for i in range(count):
                        last = tr(b[:, P * i:P * i + P], src(i), ident)
                    given(last)

                blk = [0]

                def weight_block():
                    i = blk[0]
                    blk[0] += 1
                    pe.wait_ge(w_loaded[i % 2], n * (16 * BLOCKS // 2) + 16 * (i // 2 + 1))
                    return wbuf[i % 2]

                def project_rows(full_event=True):
                    b = take()
                    for half_ in range(2):
                        wb = weight_block()
                        for k in range(KT):
                            last = mm(b[:, WB * half_:WB * half_ + WB], actT[:, k, :], wb[:, k, :],
                                      start=(k == 0), stop=(k == KT - 1))
                        if half_ == 0:
                            last.then_inc(w_free, 1)
                    given(last)
                    pe.wait_ge(full, n * len(USES) + use[0])
                    pe.sem_inc(w_free, 1)

                def project_cols():
                    b = take()
                    for half_ in range(2):
                        wb = weight_block()
                        for c in range(2):
                            o = P * (2 * half_ + c)
                            for k in range(KT):
                                last = mm(b[:, o:o + P], wb[:, k, P * c:P * c + P], actT[:, k, :],
                                          start=(k == 0), stop=(k == KT - 1))
                        if half_ == 0:
                            last.then_inc(w_free, 1)
                    given(last)
                    pe.wait_ge(full, n * len(USES) + use[0])
                    pe.sem_inc(w_free, 1)

                turn()
                pe.wait_ge(*event("x_norm", n))
                for j in range(2):
                    transposes(lambda i: rowbuf[:, P * (4 * j + i):P * (4 * j + i) + P], 4)
                turn()
                pe.wait_ge(*event("hT", n, 1))
                for j in range(3):
                    project_rows()
                    turn()
                for j in range(3):
                    project_cols()
                    turn()
                project_rows()
                turn()
                b = take()
                for k in range(KT):
                    last = mm(b[:, 0:2 * H], actT[:, k, :], w_ab_sb[:, k, :], start=(k == 0), stop=(k == KT - 1))
                given(last)
                pe.wait_ge(*event("rot", n))
                transposes(lambda i: ret_rot[:, 2 * i:2 * i + 2, :, :].rearrange("p a z d -> p (a z d)"), 4)
                turn()
                pe.wait_ge(*event("retT", n))
                pe.wait_ge(*event("ret_qd", n))
                b = take()
                for h in range(H):
                    last = mm(b[:, P * h:P * h + P], retT[:, 2 + h // 2, :], ret_qz[:, h, :], start=True, stop=True)
                given(last)
                turn()
                pe.wait_ge(*event("ret_s", n))
                pe.wait_ge(*event("vr_in", n))
                follows(pe, "ret_state", n)
                if isinstance(n, int):
                    pe.wait_ge(start_up, 3)
                b = take()
                for h in range(H):
                    mm(b[:, P * h:P * h + P], ret_s[:, h, :], v_r[:, h, :], start=True, stop=False)
                    last = mm(b[:, P * h:P * h + P], ret_qd[:, h, :], state_r[:, h // 2, :], start=False, stop=True)
                given(last)
                b = take()
                for h in range(H):
                    p0 = 64 * (h % 2)
                    last = mm(b[p0:p0 + 64, P * (h // 2):P * (h // 2) + P], ret_kd[:, h, :], v_r[:, h, :],
                              start=True, stop=True)
                given(last)
                turn()
                pe.wait_ge(*event("beta_g", n))
                b = take()
                given(mm(b[:, 0:H], causal, st[:, 20:24], start=True, stop=True))
                b = take()
                given(mm(b[:, :], ones, T[:, :, :].rearrange("p h t -> p (h t)"), start=True, stop=True))
                b = take()
                given(mm(b[:, :], ones, TT[:, :, :].rearrange("p h t -> p (h t)"), start=True, stop=True))
                pe.wait_ge(*event("sq", n))
                for j in range(2):
                    b = take()
                    given(mm(b[:, :], ones, norms[:, 4 * j:4 * j + 4, :].rearrange("p h t -> p (h t)"),
                             start=True, stop=True))
                turn()
                pe.wait_ge(*event("normed", n))
                transposes(lambda i: conv[:, 4 + i, :], 4)
                transposes(lambda i: conv[:, 8 + i, :], 4)
                turn()
                pe.wait_ge(*event("kbT", n))
                for j, rhs in ((0, kbT), (1, conv)):
                    b = take()
                    for h in range(H):
                        last = mm(b[:, P * h:P * h + P], conv[:, 4 + h, :], rhs[:, h, :], start=True, stop=True)
                    given(last)
                turn()
                pe.wait_ge(*event("NT", n))
                pe.wait_ge(*event("T_init", n))
                for i in range(LEVELS):
                    if i:
                        pe.wait_ge(*event("inv_TT", n, i - 1))
                    b = take()
                    for h in range(H):
                        last = mm(b[:, P * h:P * h + P], NT[:, h, :], T[:, h, :], start=True, stop=True)
                    given(last)
                    pe.wait_ge(*event("inv_P", n, i))
                    b = take()
                    for h in range(H):
                        last = mm(b[:, P * h:P * h + P], TT[:, h, :], Pm[:, h, :], start=True, stop=True)
                    given(last)
                    b = take()
                    for h in range(H):
                        last = mm(b[:, P * h:P * h + P], Pm[:, h, :], TT[:, h, :], start=True, stop=True)
                    given(last)
                    turn()
                pe.wait_ge(*event("inv_TT", n, LEVELS - 1))
                pe.wait_ge(*event("kbe", n))
                b = take()
                for h in range(H):
                    last = mm(b[:, P * h:P * h + P], kbe[:, h, :], TT[:, h, :], start=True, stop=True)
                given(last)
                pe.wait_ge(*event("wT", n))
                follows(pe, "gdn_state", n)
                b = take()
                for h in range(H):
                    mm(b[:, P * h:P * h + P], TT[:, h, :], vb[:, h, :], start=True, stop=False)
                    last = mm(b[:, P * h:P * h + P], wT[:, h, :], state_g[:, h, :], start=False, stop=True)
                given(last)
                turn()
                pe.wait_ge(*event("vnew", n))
                pe.wait_ge(*event("qd", n))
                b = take()
                for h in range(H):
                    mm(b[:, P * h:P * h + P], qdT[:, h, :], state_g[:, h, :], start=True, stop=False)
                    last = mm(b[:, P * h:P * h + P], attnT[:, h, :], vnew[:, h, :], start=False, stop=True)
                given(last)
                b = take()
                for h in range(H):
                    last = mm(b[:, P * h:P * h + P], kst[:, h, :], vnew[:, h, :], start=True, stop=True)
                given(last)
                turn()
                pe.wait_ge(*event("mixed", n))
                pe.wait_ge(*event("ret_mixed", n))
                for j in range(2):
                    transposes(lambda i: rowbuf[:, P * (4 * j + i):P * (4 * j + i) + P], 4)
                turn()
                pe.wait_ge(*event("mT", n, 1))
                for j in range(2):
                    project_rows()
                    turn()
                pe.wait_ge(*event("h2", n))
                for j in range(2):
                    transposes(lambda i: rowbuf[:, P * (4 * j + i):P * (4 * j + i) + P], 4)
                turn()
                pe.wait_ge(*event("h2T", n, 1))
                for j in range(4):
                    project_cols()
                    turn()
                for j in range(4):
                    pe.wait_ge(*event("qT", n, j))
                    b = take()
                    for i in range(4):
                        last = mm(b[:, P * i:P * i + P], qT[:, 4 * j + i, :], keys_sb[:, 4 * j + i, :],
                                  start=True, stop=True)
                    given(last)
                assert use[0] == len(USES) and blk[0] == BLOCKS

            pe.sem_inc(w_free, 2)
            pe.sem_inc(v_used, COUNT0)
            chunks(pe, mix, peer_turn, lambda n: None)

        @block.scalar
        def _(act):
            act.wait_ge(const_in, 16 * N_CONST)
            act.wait_ge(start_up, 3)
            A = nc.scalar.activation
            A(neg_a[:, :], a_log, ACT.Exp).then_inc(start_up, 1)

            def peer_turn(n, t):
                if t % QUARTER == 0 and 0 < t <= TURNS:
                    h = t // QUARTER - 1
                    act.wait_ge(*used(u_used, n, TOPK * h + TOPK - 1))
                    A(gelu[:, TOPK * h:TOPK * h + TOPK], dots[:, TOPK * h:TOPK * h + TOPK], ACT.Gelu
                      ).then_inc(S["gelu"], 1)
                if t % QUARTER == 1 and 1 < t <= TURNS + 1:
                    h = t // QUARTER - 1
                    act.wait_ge(*event("weight", n, h))
                    for k in range(TOPK):
                        s = TOPK * h + k
                        act.wait_ge(*used(v_used, n, s - TOPK))
                        A(diag[:, k, :], ident, ACT.Copy, scale=weight[:, s:s + 1]).then_inc(S["diag"], 1)

            def finish(n):
                act.wait_ge(*used(v_used, n, SLOTS - 1))
                A(y_sb[:, 0:512], y_ps[0][:, :], ACT.Square, accum_out=st[:, 60:61])
                A(y_sb[:, 512:1024], y_ps[1][:, :], ACT.Square, accum_out=st[:, 61:62]).then_inc(S["yss"], 1)
                act.wait_ge(*event("yms", n))
                A(st[:, 59:60], st[:, 58:59], ACT.Sqrt).then_inc(S["sqrt_y"], 1)
                act.wait_ge(S["y_out"], n + 2)
                act.dma_start(out[at(n)].rearrange("o p d -> (o p) d"), y_sb[:, :]).then_inc(y_stored, 16)
                act.wait_ge(y_stored, n * 16 + 16)

            def mix(n, turn):
                use = [0]

                def given():
                    u = use[0]
                    use[0] += 1
                    act.wait_ge(full, n * len(USES) + u + 1)
                    return bank[u % BANKS]

                def skip(k):
                    use[0] += k

                def heads(ap):
                    return ap[:, :].rearrange("p (h t) -> p h t", t=P)

                turn()
                act.wait_ge(*event("rms1", n))
                A(st[:, 1:2], st[:, 0:1], ACT.Sqrt).then_inc(S["sqrt1"], 1)
                turn()
                skip(2)
                for name, dst, f in (("qk_in", qk_r[:, :, :, :].rearrange("p h z d -> p (h z d)"), ACT.Copy),
                                     ("vr_in", v_r[:, :, :].rearrange("p h d -> p (h d)"), ACT.Copy),
                                     ("gR_in", gate_r[:, :, :].rearrange("p h d -> p (h d)"), ACT.Silu)):
                    if name == "qk_in":
                        follows(act, "ret_qd", n)
                    if name == "vr_in":
                        follows(act, "ret_state", n)
                    if name == "gR_in":
                        follows(act, "ret_mixed", n)
                    A(dst, given()[:, :], f).then_inc(S[name], 1)
                    turn()
                follows(act, "conv_done", n)
                for j in range(3):
                    A(conv_in[:, 4 * j:4 * j + 4, 3:P + 3], heads(given()), ACT.Copy).then_inc(S["conv_in"], 1)
                    turn()
                follows(act, "mixed", n)
                A(gate_g[:, :, :].rearrange("p h d -> p (h d)"), given()[:, :], ACT.Silu).then_inc(S["gG_in"], 1)
                turn()
                skip(1)
                A(retT[:, :, :], heads(given()), ACT.Copy).then_inc(S["retT"], 1)
                turn()
                skip(1)
                act.wait_ge(*event("sp_in", n))
                A(st[:, 8:12], st[:, 4:8], ACT.Exp)
                A(st[:, 12:16], ab[:, 1, :], ACT.Exp, scale=-1.0).then_inc(S["exp_ab"], 1)
                act.wait_ge(*event("exp_ab", n))
                A(st[:, 16:20], st[:, 8:12], ACT.Ln, bias=1.0).then_inc(S["ln_ab"], 1)
                turn()
                skip(2)
                act.wait_ge(*event("ret_out_ready", n))
                A(st[:, 28:32], mv[:, :, 1], ACT.Sqrt, bias=eps_col[:, 0:1]).then_inc(S["sqrt_ret"], 1)
                turn()
                act.wait_ge(*event("conv_done", n))
                A(conv[:, :, :], conv[:, :, :], ACT.Silu).then_inc(S["silu_conv"], 1)
                act.wait_ge(*event("silu_conv", n))
                A(norms[:, :, :], conv[:, 0:8, :], ACT.Square).then_inc(S["sq"], 1)
                skip(1)
                act.wait_ge(*event("diff", n))
                A(cmask[:, :, :], cmask[:, :, :], ACT.Exp)
                A(st[:, 36:44], st[:, 44:52], ACT.Exp).then_inc(S["exp_diff"], 1)
                A(expg[:, :, :], heads(given()), ACT.Exp).then_inc(S["E"], 1)
                skip(1)
                for j in range(2):
                    b = given()
                    A(norms[:, 4 * j:4 * j + 4, :], heads(b), ACT.Sqrt, bias=eps_col[:, 0:1]).then_inc(S["norm_in"], 1)
                turn()
                skip(2)
                turn()
                skip(2)
                turn()
                for i in range(LEVELS):
                    skip(3)
                    turn()
                A(wT[:, :, :], heads(given()), ACT.Copy, scale=-1.0).then_inc(S["wT"], 1)
                A(vnew[:, :, :], heads(given()), ACT.Copy).then_inc(S["vnew"], 1)
                turn()
                b = given()
                for h in range(H):
                    last = A(qdT[:, h, :], b[:, P * h:P * h + P], ACT.Square, accum_out=st[:, 52 + h:53 + h])
                last.then_inc(S["gdn_ss"], 1)
                skip(1)
                act.wait_ge(*event("gdn_ms", n))
                A(st[:, 32:36], st[:, 24:28], ACT.Sqrt).then_inc(S["sqrt_gdn"], 1)
                turn()
                for j in range(2):
                    A(actT[:, 4 * j:4 * j + 4, :], heads(given()), ACT.Copy).then_inc(S["mT"], 1)
                turn()
                turn()
                turn()
                skip(2)
                act.wait_ge(*event("rms2", n))
                A(st[:, 1:2], st[:, 0:1], ACT.Sqrt).then_inc(S["sqrt2"], 1)
                for j in range(2):
                    A(actT[:, 4 * j:4 * j + 4, :], heads(given()), ACT.Copy).then_inc(S["h2T"], 1)
                turn()
                for j in range(4):
                    A(qT[:, 4 * j:4 * j + 4, :], heads(given()), ACT.Copy).then_inc(S["qT"], 1)
                    turn()
                for j in range(4):
                    A(scores[:, 4 * j:4 * j + 4, :], heads(given()), ACT.Copy).then_inc(S["scores"], 1)
                turn()
                act.wait_ge(*event("gate_in", n))
                A(best[:, :, :], best[:, :, :], ACT.Exp).then_inc(S["gate_exp"], 1)
                assert use[0] == len(USES)

            chunks(act, mix, peer_turn, finish)

        @block.vector
        def _(dve):
            V = nc.vector
            MIX_LINKS, PEER_LINKS = 45, 3
            V.memset(state_g[:, :, :], 0.0)
            V.memset(state_r[:, :, :], 0.0)
            V.memset(conv_in[:, :, 0:3], 0.0)
            dve.wait_ge(start_up, 2)
            V.memset(eps_col[:, :], EPS).then_inc(start_up, 1)
            dve.wait_ge(start_up, 4)
            V.tensor_scalar(neg_a[:, :], neg_a[:, :], -1.0, None, ALU.mult).then_inc(start_up, 1)
            dve.wait_ge(start_up, 5)
            dve.wait_ge(const_in, 16 * N_CONST)
            dve.sem_inc(u_used, COUNT0)
            dve.sem_inc(S["y_out"], 1)

            def peer_turn(n, t):
                if t == 0:
                    V.tensor_copy(h2[:, :], rowbuf[:, :])
                    V.tensor_copy(gate[:, :], gate_next[:, :])
                    dve.wait_ge(*used(v_used, n, -LATE * TOPK - 1))
                    V.tensor_copy(ids[:, 0:SLOTS - LATE * TOPK], ids_next[:, 0:SLOTS - LATE * TOPK]
                                  ).then_inc(S["peer_in"], 1)
                    dve.wait_ge(*event("peer_in", n))
                if t == LAG:
                    dve.wait_ge(*used(v_used, n, -1))
                    V.tensor_copy(ids[:, SLOTS - LATE * TOPK:], ids_next[:, SLOTS - LATE * TOPK:]
                                  ).then_inc(S["ids_late"], 1)
                if t < TURNS:
                    for s in range(QUARTER * t, QUARTER * t + QUARTER):
                        u = urow[s % RING][:, :]
                        dve.wait_ge(u_loaded[s % RING], n * (16 * SLOTS // RING) + 16 * (s // RING + 1))
                        V.tensor_tensor_reduce(out=u, in0=u, in1=h2[:, :], scale=1.0, scalar=0.0, op0=ALU.mult,
                                               op1=ALU.add, accum_out=dots[:, s:s + 1]).then_inc(u_used, 1)
                if t % QUARTER == 0 and 0 < t <= TURNS:
                    h = t // QUARTER - 1
                    c0, c1 = TOPK * h, TOPK * h + TOPK
                    dve.wait_ge(*event("gelu", n, h))
                    V.tensor_tensor(weight[:, c0:c1], gelu[:, c0:c1], gate[:, c0:c1], ALU.mult).then_inc(S["weight"], 1)

            def finish(n):
                base = n * PEER_LINKS
                dve.wait_ge(*event("yss", n))
                V.tensor_tensor(st[:, 57:58], st[:, 60:61], st[:, 61:62], ALU.add).then_inc(peer_chain, 1)
                dve.wait_ge(peer_chain, base + 1)
                V.tensor_scalar(st[:, 58:59], st[:, 57:58], 1.0 / D, EPS, ALU.mult, ALU.add).then_inc(S["yms"], 1)
                dve.wait_ge(*event("sqrt_y", n))
                V.reciprocal(st[:, 57:58], st[:, 59:60]).then_inc(peer_chain, 1)
                dve.wait_ge(peer_chain, base + 2)
                V.scalar_tensor_tensor(y_sb[:, 0:512], y_ps[0][:, :], st[:, 57:58], lnf_row[:, 0:512],
                                       ALU.mult, ALU.mult).then_inc(peer_chain, 1)
                V.scalar_tensor_tensor(y_sb[:, 512:1024], y_ps[1][:, :], st[:, 57:58], lnf_row[:, 512:1024],
                                       ALU.mult, ALU.mult).then_inc(S["y_out"], 1)

            def mix(n, turn):
                use, links = [0], [0]

                def given():
                    u = use[0]
                    use[0] += 1
                    dve.wait_ge(full, n * len(USES) + u + 1)
                    return bank[u % BANKS]

                def skip(k):
                    use[0] += k

                def link(ins, apart=False):
                    links[0] += 1
                    ins.then_inc(mix_chain, 1)
                    dve.wait_ge(mix_chain, n * MIX_LINKS + links[0])
                    if apart:
                        dve.sem_inc(passed, 1)

                def heads(ap):
                    return ap[:, :].rearrange("p (h t) -> p h t", t=P)

                def by_head(ap, k=P):
                    return ap.unsqueeze(2).broadcast_to([P, ap.shape[1], k])

                def each_head(ap):
                    return ap.unsqueeze(1).broadcast_to([P, H, P])

                turn()
                dve.wait_ge(x_loaded, n * 16 + 16)
                link(V.tensor_tensor_reduce(out=rowbuf[:, :], in0=x_in[:, :], in1=x_in[:, :], scale=1.0, scalar=0.0,
                                            op0=ALU.mult, op1=ALU.add, accum_out=st[:, 2:3]))
                V.tensor_scalar(st[:, 0:1], st[:, 2:3], 1.0 / D, EPS, ALU.mult, ALU.add).then_inc(S["rms1"], 1)
                dve.wait_ge(*event("sqrt1", n))
                link(V.reciprocal(st[:, 2:3], st[:, 1:2]))
                V.tensor_scalar(rowbuf[:, :], x_in[:, :], st[:, 2:3], None, ALU.mult).then_inc(S["x_norm"], 1)
                turn()
                for j in range(2):
                    V.tensor_tensor(actT[:, 4 * j:4 * j + 4, :], heads(given()), by_head(lnT[:, 4 * j:4 * j + 4]),
                                    ALU.mult).then_inc(S["hT"], 1)
                skip(3)
                turn()
                dve.wait_ge(*event("qk_in", n))
                q1, q2 = qk_r[:, :, 0, :], qk_r[:, :, 1, :]
                cos, sin, nsin = (ropes[:, i, at(n), :]
                                  .broadcast_to([P, 2 * H, 32]) for i in range(3))
                V.tensor_tensor(ret_rot[:, :, 0, :], q1, cos, ALU.mult)
                V.tensor_tensor(ret_rot[:, :, 1, :], q2, cos, ALU.mult)
                V.tensor_tensor(ret_tmp[:, :, 0, :], q2, nsin, ALU.mult)
                link(V.tensor_tensor(ret_tmp[:, :, 1, :], q1, sin, ALU.mult))
                V.tensor_tensor(ret_rot[:, :, :, :], ret_rot[:, :, :, :], ret_tmp[:, :, :, :], ALU.add
                                ).then_inc(S["rot"], 1)
                dve.wait_ge(*event("rot", n))
                V.tensor_tensor(ret_kd[:, :, :], ret_rot[:, H:2 * H, :, :].rearrange("p h z d -> p h (z d)"),
                                by_head(smalls[:, 0:4], 64), ALU.mult)
                for _ in range(6):
                    turn()
                use[0] += 4
                link(V.tensor_copy(ab[:, :, :].rearrange("p a h -> p (a h)"), given()[:, 0:2 * H]))
                V.tensor_copy(st[:, 3:4], ab[:, 0, 0:1]).then_inc(S["ab_in"], 1)
                link(V.tensor_tensor(st[:, 52:56], ab[:, 0, :], dt_bias, ALU.add))
                link(V.tensor_scalar(st[:, 4:8], st[:, 52:56], -1.0, None, ALU.mult))
                V.tensor_tensor(st[:, 4:8], st[:, 4:8], st[:, 52:56], ALU.min).then_inc(S["sp_in"], 1)
                turn()
                dve.wait_ge(*event("retT", n))
                for h in range(H):
                    V.tensor_scalar(ret_qz[:, h, :], retT[:, h // 2, :], smalls[:, 6 + h:7 + h], None, ALU.mult)
                    last = V.tensor_tensor(ret_qd[:, h, :], retT[:, h // 2, :], ret_qdec[:, h, :], ALU.mult)
                last.then_inc(S["ret_qd"], 1)
                skip(1)
                V.tensor_tensor(ret_s[:, :, :], heads(given()), ret_decay, ALU.mult).then_inc(S["ret_s"], 1)
                turn()
                b = given()
                for h in range(H):
                    last = V.bn_stats(bn[:, h, :], b[:, P * h:P * h + P])
                link(last, apart=True)
                for h in range(H):
                    last = V.bn_aggr(mv[:, h, :], bn[:, h, :])
                last.then_inc(S["ret_out_ready"], 1)
                dve.wait_ge(*event("ln_ab", n))
                link(V.tensor_scalar(st[:, 4:8], st[:, 52:56], 0.0, None, ALU.max))
                V.tensor_scalar(st[:, 12:16], st[:, 12:16], 1.0, None, ALU.add)
                link(V.tensor_tensor(st[:, 4:8], st[:, 4:8], st[:, 16:20], ALU.add))
                V.tensor_tensor(st[:, 20:24], st[:, 4:8], neg_a[:, :], ALU.mult)
                link(V.reciprocal(st[:, 48:52], st[:, 12:16]))
                V.tensor_tensor(T[:, :, :], each_head(causal), by_head(st[:, 20:24]), ALU.mult)
                V.tensor_tensor(TT[:, :, :], each_head(ident), by_head(st[:, 48:52]), ALU.mult).then_inc(S["beta_g"], 1)
                dve.wait_ge(*event("sqrt_ret", n))
                V.tensor_tensor(gate_r[:, :, :].rearrange("p h d -> p (h d)"),
                                gate_r[:, :, :].rearrange("p h d -> p (h d)"), retw_row, ALU.mult)
                link(V.reciprocal(st[:, 32:36], st[:, 28:32]))
                for h in range(H):
                    last = V.tensor_scalar(ret_s[:, h, :], b[:, P * h:P * h + P], mv[:, h, 0:1], st[:, 32 + h:33 + h],
                                           ALU.subtract, ALU.mult)
                last.then_inc(S["ret_norm"], 1)
                dve.wait_ge(*event("ret_norm", n))
                V.tensor_tensor(rowbuf[:, 0:512], ret_s[:, :, :].rearrange("p h d -> p (h d)"),
                                gate_r[:, :, :].rearrange("p h d -> p (h d)"), ALU.mult).then_inc(S["ret_mixed"], 1)
                b = given()
                for j in range(2):
                    last = V.scalar_tensor_tensor(state_r[:, j, :], state_r[:, j, :], smalls[:, 4 + j:5 + j],
                                                  b[:, P * j:P * j + P], ALU.mult, ALU.add)
                last.then_inc(S["ret_state"], 1)
                turn()
                dve.wait_ge(*event("conv_in", n, 2))
                for j in range(4):
                    for c in range(12):
                        src = conv_in[:, c, j:j + P]
                        if j == 0:
                            last = V.tensor_scalar(conv[:, c, :], src, conv_w[:, c, 0:1], None, ALU.mult)
                        else:
                            last = V.scalar_tensor_tensor(conv[:, c, :], src, conv_w[:, c, j:j + 1], conv[:, c, :],
                                                          ALU.mult, ALU.add)
                    link(last)
                V.tensor_copy(conv_in[:, :, 0:3], conv_in[:, :, P:P + 3]).then_inc(S["conv_done"], 1)
                link(V.tensor_copy(st[:, 44:48], given()[:, 0:H]))
                V.tensor_copy(st[:, 3:4], st[:, 44:45]).then_inc(S["gc_in"], 1)
                b = given()
                for h in range(H):
                    V.tensor_scalar(cmask[:, h, :], b[:, P * h:P * h + P], st[:, 44 + h:45 + h], 0.0,
                                    ALU.subtract, ALU.min)
                link(V.tensor_copy(st[:, 24:28], st[:, 48:52]))
                V.tensor_tensor(st[:, 48:52], heads(b)[:, :, P - 1], st[:, 44:48], ALU.subtract).then_inc(S["diff"], 1)
                dve.wait_ge(*event("exp_diff", n))
                link(V.tensor_tensor(st[:, 36:40], st[:, 36:40], st[:, 24:28], ALU.mult))
                link(V.tensor_tensor(cmask[:, :, :], cmask[:, :, :], each_head(causal), ALU.mult))
                beta_row = given()
                dve.wait_ge(*event("norm_in", n, 1))
                link(V.reciprocal(norms[:, :, :], norms[:, :, :]))
                V.scalar_tensor_tensor(conv[:, 0:4, :].rearrange("p h t -> p (h t)"),
                                       conv[:, 0:4, :].rearrange("p h t -> p (h t)"), float(DV) ** -0.5,
                                       norms[:, 0:4, :].rearrange("p h t -> p (h t)"), ALU.mult, ALU.mult)
                V.tensor_tensor(conv[:, 4:8, :], conv[:, 4:8, :], norms[:, 4:8, :], ALU.mult).then_inc(S["normed"], 1)
                dve.wait_ge(*event("normed", n))
                V.tensor_tensor(kbT[:, :, :], conv[:, 4:8, :], heads(beta_row), ALU.mult).then_inc(S["kbT"], 1)
                skip(2)
                dve.wait_ge(*event("E", n))
                V.tensor_tensor(qdT[:, :, :], conv[:, 0:4, :], expg[:, :, :], ALU.mult).then_inc(S["qd"], 1)
                turn()
                b = given()
                V.tensor_tensor(kbe[:, :, :], heads(b), by_head(st[:, 36:40]), ALU.mult).then_inc(S["kbe"], 1)
                V.tensor_tensor(kst[:, :, :], heads(b), by_head(st[:, 40:44]), ALU.mult).then_inc(S["kst"], 1)
                V.tensor_tensor(vb[:, :, :], heads(given()), by_head(st[:, 24:28]), ALU.mult).then_inc(S["vb"], 1)
                V.tensor_copy(T[:, :, :], each_head(ident))
                V.tensor_copy(TT[:, :, :], each_head(ident)).then_inc(S["T_init"], 1)
                turn()
                b, b2 = given(), given()
                link(V.tensor_tensor(NT[:, :, :], heads(b), cmask[:, :, :], ALU.mult))
                V.tensor_tensor(NT[:, :, :], NT[:, :, :], each_head(strict), ALU.mult).then_inc(S["NT"], 1)
                V.tensor_tensor(attnT[:, :, :], heads(b2), cmask[:, :, :], ALU.mult).then_inc(S["attn"], 1)
                turn()
                for i in range(LEVELS):
                    V.tensor_tensor(Pm[:, :, :], heads(given()), each_head(level_mask[i]), ALU.mult
                                    ).then_inc(S["inv_P"], 1)
                    b, b2 = given(), given()
                    dve.wait_ge(full, n * len(USES) + use[0])
                    V.tensor_tensor(T[:, :, :], T[:, :, :], heads(b), ALU.subtract).then_inc(S["inv_T"], 1)
                    V.tensor_tensor(TT[:, :, :], TT[:, :, :], heads(b2), ALU.subtract).then_inc(S["inv_TT"], 1)
                    turn()
                skip(2)
                turn()
                b, b2 = given(), given()
                dve.wait_ge(*event("gdn_ss", n))
                V.tensor_scalar(st[:, 24:28], st[:, 52:56], 1.0 / DV, EPS, ALU.mult, ALU.add).then_inc(S["gdn_ms"], 1)
                dve.wait_ge(full, n * len(USES) + use[0])
                for h in range(H):
                    last = V.scalar_tensor_tensor(state_g[:, h, :], state_g[:, h, :], expg[:, h, P - 1:P],
                                                  b2[:, P * h:P * h + P], ALU.mult, ALU.add)
                last.then_inc(S["gdn_state"], 1)
                dve.wait_ge(*event("gG_in", n))
                link(V.tensor_tensor(gate_g[:, :, :], gate_g[:, :, :], each_head(gdnw_row), ALU.mult))
                dve.wait_ge(*event("sqrt_gdn", n))
                link(V.reciprocal(st[:, 28:32], st[:, 32:36]))
                for h in range(H):
                    last = V.scalar_tensor_tensor(rowbuf[:, 512 + P * h:512 + P * h + P], b[:, P * h:P * h + P],
                                                  st[:, 28 + h:29 + h], gate_g[:, h, :], ALU.mult, ALU.mult)
                last.then_inc(S["gdn_norm"], 1)
                V.tensor_copy(st[:, 3:4], st[:, 28:29]).then_inc(S["mixed"], 1)
                turn()
                turn()
                skip(2)
                for j in range(2):
                    b = given()
                    if j == 0 and (not isinstance(n, int) or n > 0):
                        dve.wait_ge(*used(v_used, n - 1, 0))
                    V.tensor_tensor(x2[:, 512 * j:512 * j + 512], b[:, :], x_in[:, 512 * j:512 * j + 512], ALU.add
                                    ).then_inc(S["x2"], 1)
                    turn()
                dve.wait_ge(*event("x2", n, 1))
                link(V.tensor_tensor_reduce(out=rowbuf[:, :], in0=x2[:, :], in1=x2[:, :], scale=1.0, scalar=0.0,
                                            op0=ALU.mult, op1=ALU.add, accum_out=st[:, 2:3]))
                V.tensor_scalar(st[:, 0:1], st[:, 2:3], 1.0 / D, EPS, ALU.mult, ALU.add).then_inc(S["rms2"], 1)
                dve.wait_ge(*event("sqrt2", n))
                link(V.reciprocal(st[:, 2:3], st[:, 1:2]))
                V.scalar_tensor_tensor(rowbuf[:, :], x2[:, :], st[:, 2:3], ln2_row, ALU.mult, ALU.mult
                                       ).then_inc(S["h2"], 1)
                turn()
                skip(6)
                for j in range(4):
                    turn()
                dve.wait_ge(*event("scores", n, 3))
                dve.sem_inc(passed, 1)
                skip(4)

                def top16(count, src, vals, index):
                    for part in range(2):
                        o = 8 * part
                        for t in range(count):
                            last = V.max(vals(t)[:, o:o + 8], src(t))
                        link(last, apart=True)
                        for t in range(count):
                            last = V.max_index(index(t)[:, o:o + 8], vals(t)[:, o:o + 8], src(t))
                        if part == 0:
                            for t in range(count):
                                last = V.match_replace(src(t), vals(t)[:, 0:8], src(t), LOWEST)
                        link(last, apart=True)
                        turn()

                top16(16, lambda t: scores[:, t, :], lambda t: top_v[:, t, :], lambda t: top_i[:, t, :])
                V.tensor_copy(top_if[:, :, :], top_i[:, :, :])
                for h in range(PH):
                    last = V.tensor_tensor(
                        cand[:, h, :].rearrange("p (a b) -> p a b", b=TOPK),
                        top_v[:, 2 * h, :].unsqueeze(2).broadcast_to([P, TOPK, TOPK]),
                        top_v[:, 2 * h + 1, :].unsqueeze(1).broadcast_to([P, TOPK, TOPK]), ALU.add)
                link(last, apart=True)
                top16(PH, lambda t: cand[:, t, :], lambda t: best[:, t, :], lambda t: pos[:, TOPK * t:TOPK * t + TOPK])
                V.tensor_scalar(pos2[:, 0, :], pos[:, :], 4, None, ALU.logical_shift_right)
                link(V.tensor_scalar(pos2[:, 1, :], pos[:, :], TOPK - 1, None, ALU.bitwise_and))
                link(V.tensor_copy(pos_f[:, :, :], pos2[:, :, :]))
                link(V.tensor_copy(st[:, 52:60], best[:, :, 0]))
                V.tensor_tensor(best[:, :, :], best[:, :, :], by_head(st[:, 52:60], TOPK), ALU.subtract
                                ).then_inc(S["gate_in"], 1)
                iota_all = iota_f[:, :].unsqueeze(1).broadcast_to([P, SLOTS, TOPK])
                for z in range(2):
                    link(V.tensor_tensor(picked[:, :, :], by_head(pos_f[:, z, :], TOPK), iota_all, ALU.is_equal))
                    for h in range(PH):
                        last = V.tensor_tensor(picked[:, TOPK * h:TOPK * h + TOPK, :], picked[:, TOPK * h:TOPK * h + TOPK, :],
                                               top_if[:, 2 * h + z, :].unsqueeze(1).broadcast_to([P, TOPK, TOPK]), ALU.mult)
                    link(last)
                    link(V.tensor_reduce(sel[:, z, :], picked[:, :, :], AX, ALU.add))
                V.scalar_tensor_tensor(ids_next[:, :], sel[:, 0, :], float(KEYS), sel[:, 1, :], ALU.mult, ALU.add)
                dve.wait_ge(*event("gate_exp", n))
                link(V.tensor_reduce(st[:, 52:60], best[:, :, :], AX, ALU.add))
                link(V.reciprocal(st[:, 52:60], st[:, 52:60]))
                V.tensor_tensor(gate_next[:, :].rearrange("p (h k) -> p h k", k=TOPK), best[:, :, :],
                                by_head(st[:, 52:60], TOPK), ALU.mult).then_inc(S["routed"], 1)
                dve.wait_ge(*event("routed", n))
                assert links[0] == MIX_LINKS, links
                assert use[0] == len(USES), use

            chunks(dve, mix, peer_turn, finish)


def at(n):
    return slice(n, n + 1) if isinstance(n, int) else bass.ds(n, 1)


def chunks(eng, mix, peer_turn, finish):
    def together(n, first=False, mixing=True):
        t = [0]

        def turn():
            if t[0] < TURNS + LAG:
                if t[0] == LAG - 1 and not first:
                    finish(n - 1)
                peer_turn(n, t[0])
                t[0] += 1

        if mixing:
            mix(n + 1, turn)
        while t[0] < TURNS + LAG:
            turn()

    mix(0, lambda: None)
    together(0, first=True)
    with eng.Fori(1, NCH - 1) as n:
        together(n)
    together(NCH - 1, mixing=False)
    finish(NCH - 1)


def shape_tables():
    i = np.arange(P)
    tables = np.zeros((P, TAB, P), np.float32)
    tables[:, 0] = np.eye(P)
    tables[:, 1] = i[:, None] <= i[None, :]
    tables[:, 2] = i[:, None] < i[None, :]
    tables[:, 3] = 1.0
    for l in range(LEVELS):
        r, c = i[:, None] >> l, i[None, :] >> l
        tables[:, 4 + l] = (r % 2 == 1) & (c == r - 1)
    lg = np.log1p(-np.exp2(-5.0 - np.arange(H)))
    diff = (i[None, :] - i[:, None]).astype(np.float64)
    for h in range(H):
        tables[:, 4 + LEVELS + h] = np.where(diff >= 0, np.exp(lg[h] * np.maximum(diff, 0)), 0) * 64 ** -0.5
    inv = np.float32(10000.0) ** (-np.arange(32, dtype=np.float32) / np.float32(32))
    ang = (np.arange(SEQ, dtype=np.float32)[:, None] * inv[None, :].astype(np.float32)).reshape(NCH, P, 32)
    ang = ang.transpose(1, 0, 2).astype(np.float64)
    rope = np.stack([np.cos(ang), np.sin(ang), -np.sin(ang)], 1).astype(np.float32)
    of = np.array([[2 * j + p // 64 for j in range(2)] for p in range(P)])
    here = (np.arange(H)[None, :] % 2 == i[:, None] // 64).astype(np.float64)
    qdec = (np.exp(lg[:, None] * (i + 1.0)[None, :])[None] * here[:, :, None]).astype(np.float32)
    small = np.concatenate([np.exp(lg[None, :] * (P - 1.0 - i)[:, None]) * 64 ** -0.5, np.exp(lg[of] * P), here], 1)
    return tables, rope, qdec, np.ascontiguousarray(small, np.float32)


def kernel(**inputs):
    import concourse.bacc as bacc
    from concourse.bass_utils import run_bass_kernel_spmd

    a = {k: np.asarray(v) for k, v in inputs.items()}

    def tiles(m, block):
        return m.reshape(KT, P, -1, block).transpose(2, 1, 0, 3)

    w_in = a["w_in"][0]
    w = np.concatenate([tiles(w_in[:, 0:IN_BLOCKS * WB], WB), tiles(a["w_out"][0], WB), tiles(a["peer_wq"][0], WB)])
    w_ab = tiles(w_in[:, IN_BLOCKS * WB:], 2 * H)[0]
    cols = np.concatenate([a["ln1_w"][0].reshape(KT, P).T,
                           a["conv_w"][0].reshape(4, 12, P).transpose(2, 1, 0).reshape(P, 48)], 1)
    head_rows = np.concatenate([a["ret_norm_w"][0], a["gdn_norm_w"][0], a["A_log"][0], a["dt_bias"][0]])
    tables, rope, qdec, small = shape_tables()
    arrays = {
        "x": a["x"].reshape(NCH, P, D), "w": w, "w_ab": w_ab,
        "keysT": a["peer_keys"][0].reshape(16, KEYS, P).transpose(2, 0, 1),
        "u_tab": a["peer_u"][0], "v_tab": a["peer_v"][0], "cols": cols,
        "rows": np.stack([a["ln2_w"][0], a["lnf_w"]]), "head_rows": head_rows,
        "tables": tables, "rope": rope, "qdec": qdec, "small": small,
    }
    nc = bacc.Bacc("TRN2", target_bir_lowering=False, num_devices=1)
    arrays = {k: np.ascontiguousarray(v) for k, v in arrays.items()}
    args = [nc.dram_tensor(k, v.shape, mybir.dt.from_np(v.dtype), kind="ExternalInput").ap() for k, v in arrays.items()]
    args.append(nc.dram_tensor("y", (NCH, P, D), F32, kind="ExternalOutput").ap())
    build(nc, *args)
    r = run_bass_kernel_spmd(nc, [arrays], core_ids=[0])
    return r.results[0]["y"].reshape(1, SEQ, D)
```

```python
from contextlib import ExitStack

import concourse.bass as bass
import numpy as np
from concourse import mybir

ALU = mybir.AluOpType
ACT = mybir.ActivationFunctionType
AX = mybir.AxisListType.X
F32 = mybir.dt.float32
U32 = mybir.dt.uint32

P = 128
D = 1024
KT = D // P
SEQ = 1024
NCH = SEQ // P
H = 4
DV = 128
EPS = 1e-6
WB = 256
IN_BLOCKS, OUT_BLOCKS, Q_BLOCKS = 14, 4, 8
BLOCKS = IN_BLOCKS + OUT_BLOCKS + Q_BLOCKS
PH, TOPK, KEYS = 8, 16, 128
SLOTS = PH * TOPK
QUARTER = 4
TURNS = SLOTS // QUARTER
LAG = 6
RING = 8
LEVELS = 7
LOWEST = -3.0e38
COUNT0 = 64
LATE = 2
TAB = 1 + 1 + 1 + 1 + LEVELS + H

USES = (
    [("xT0", "hT", 2, 0), ("xT1", "hT", 2, 1), ("ab", "ab_in", 1, 0), ("gq", "conv_in", 3, 0),
     ("gk", "conv_in", 3, 1), ("gv", "conv_in", 3, 2), ("gc", "gc_in", 1, 0), ("gc_row", "E", 1, 0),
     ("beta_row", "kbT", 1, 0), ("rqk", "qk_in", 1, 0), ("ssq", "norm_in", 2, 0), ("ssk", "norm_in", 2, 1),
     ("rv", "vr_in", 1, 0), ("kT", "kst", 1, 0), ("vT", "vb", 1, 0), ("kk", "NT", 1, 0), ("qk", "attn", 1, 0),
     ("rg", "gR_in", 1, 0)]
    + [u for i in range(LEVELS) for u in (
        [(f"P{i}", "inv_P", LEVELS, i)]
        + {0: [("gz", "gG_in", 1, 0)], 1: [("retT", "retT", 1, 0)], 2: [("ret_s", "ret_s", 1, 0)],
           3: [("ret_out", "ret_norm", 1, 0), ("ret_kv", "ret_state", 1, 0)]}.get(i, [])
        + [(f"Q{i}", "inv_T", LEVELS, i), (f"R{i}", "inv_TT", LEVELS, i)])]
    + [("wT", "wT", 1, 0), ("vnew", "vnew", 1, 0), ("gdn_out", "gdn_norm", 1, 0), ("gdn_kv", "gdn_state", 1, 0),
       ("mT0", "mT", 2, 0), ("mT1", "mT", 2, 1), ("out0", "x2", 2, 0), ("out1", "x2", 2, 1),
       ("h2T0", "h2T", 2, 0), ("h2T1", "h2T", 2, 1)]
    + [(f"q{i}", "qT", 4, i) for i in range(4)] + [(f"s{i}", "scores", 4, i) for i in range(4)]
)
PLACE = {u[0]: i for i, u in enumerate(USES)}
BANKS = 6
PACE = [1, 1, 1, 1, 1, 0, 1, 1, 1, 1, 1, 1, 0, 1, 0, 1, 0, 1, 0, 1, 0, 1, 0, 1, 0, 1, 1, 1, 1, 1, 1, 1, 1, 0, 1, 0,
        1, 1, 1, 1, 1, 1, 0, 0]
NUSE = -(-len(USES) // BANKS) * BANKS


def build(nc, x, w, w_ab, keysT, u_tab, v_tab, cols, rows, head_rows, tables, rope, qdec, small, out):
    with ExitStack() as ctx:
        def sb(name, shape, dt=F32):
            return ctx.enter_context(nc.sbuf_tensor(name, [P, *shape], dt))

        def sem(name):
            return ctx.enter_context(nc.semaphore(name))

        tab = sb("tab", [TAB, P])
        ident, causal, strict, ones = (tab[:, i, :] for i in range(4))
        level_mask = [tab[:, 4 + i, :] for i in range(LEVELS)]
        ret_decay = tab[:, 4 + LEVELS:4 + LEVELS + H, :]
        ropes = sb("ropes", [3, NCH, 32])
        ret_qdec = sb("ret_qdec", [H, P])
        smalls = sb("smalls", [10])
        lnT = sb("lnT", [KT])
        conv_w = sb("conv_w", [12, 4])
        rowsb = sb("rowsb", [2, D])
        ln2_row, lnf_row = rowsb[:, 0, :], rowsb[:, 1, :]
        headsb = sb("headsb", [5 * P + 2 * H])
        retw_row, gdnw_row = headsb[:, 0:512], headsb[:, 512:640]
        a_log, dt_bias = headsb[:, 640:644], headsb[:, 644:648]
        neg_a = sb("neg_a", [H])
        eps_col = sb("eps_col", [1])
        w_ab_sb = sb("w_ab_sb", [KT, 2 * H])
        keys_sb = sb("keys_sb", [16, P])

        wbuf = [sb(f"wbuf{i}", [KT, WB]) for i in range(2)]
        x_in = sb("x_in", [D])
        x2 = sb("x2_row", [D])
        rowbuf = sb("rowbuf", [D])
        actT = sb("actT", [KT, P])
        qk_r = sb("qk_r", [2 * H, 2, 32])
        v_r = sb("v_r", [H, DV])
        gate_r = sb("gate_r", [H, DV])
        gate_g = sb("gate_g", [H, DV])
        ab = sb("ab", [2, H])
        conv_in = sb("conv_in", [12, P + 3])
        area = sb("area", [10, 256])
        ret_rot = area[:, 0:2, :].rearrange("p a (h z d) -> p (a h) z d", z=2, d=32)
        ret_tmp = area[:, 2:4, :].rearrange("p a (h z d) -> p (a h) z d", z=2, d=32)
        retT = area[:, 4:6, :].rearrange("p a (b t) -> p (a b) t", t=P)
        ret_qz = area[:, 2:4, :].rearrange("p a (b t) -> p (a b) t", t=P)
        ret_qd = area[:, 0:2, :].rearrange("p a (b t) -> p (a b) t", t=P)
        ret_kd = area[:, 7, :].rearrange("p (h d) -> p h d", d=64)
        ret_s = area[:, 8:10, :].rearrange("p a (b t) -> p (a b) t", t=P)
        flat = area[:, :, :].rearrange("p a b -> p (a b)")
        conv = flat[:, 0:1536].rearrange("p (c t) -> p c t", t=P)
        norms = flat[:, 1536:2560].rearrange("p (c t) -> p c t", t=P)
        cmask = sb("decayT", [H, P])
        expg = sb("expg", [H, P])
        vb = sb("vb", [H, DV])
        kst = sb("kst", [H, P])
        vnew = sb("vnew", [H, DV])
        qdT = sb("qdT", [H, P])
        state_g = sb("state_g", [H, DV])
        state_r = sb("state_r", [2, DV])
        arena = sb("arena", [16, 256])
        half = lambda i: arena[:, 2 * i:2 * i + 2, :].rearrange("p a (b t) -> p (a b) t", t=P)
        NT, attnT, T, TT, Pm, kbe, wT, kbT = (half(i) for i in range(8))
        qT = arena[:, 0:8, :].rearrange("p a (b t) -> p (a b) t", t=P)
        scores = arena[:, 8:16, :].rearrange("p a (b t) -> p (a b) t", t=P)
        cand = qT.rearrange("p (h z) t -> p h (z t)", z=2)
        picked = scores.rearrange("p a (b t) -> p (a b) t", t=TOPK)
        st = sb("st", [64])
        bn = sb("bn", [H, 6])
        mv = sb("mv", [H, 2])
        top_v = sb("top_v", [16, TOPK])
        top_i = sb("top_i", [16, TOPK], U32)
        top_if = sb("top_if", [16, TOPK])
        best = sb("best", [PH, TOPK])
        pos = sb("pos", [SLOTS], U32)
        pos2 = sb("pos2", [2, SLOTS], U32)
        pos_f = sb("pos_f", [2, SLOTS])
        sel = sb("sel", [2, SLOTS])
        gate_next = sb("gate_next", [SLOTS])
        ids_next = sb("ids_next", [SLOTS])
        iota_f = sb("iota_f", [TOPK])

        urow = [sb(f"urow{i}", [D]) for i in range(RING)]
        vrow = [sb(f"vrow{i}", [D]) for i in range(RING)]
        h2 = sb("h2", [D])
        ids = sb("ids", [SLOTS], U32)
        gate = sb("gate", [SLOTS])
        dots = sb("dots", [SLOTS])
        gelu = sb("gelu", [SLOTS])
        weight = sb("weight", [SLOTS])
        diag = sb("diag", [TOPK, P])
        y_sb = diag[:, 0:D // P, :].rearrange("p k t -> p (k t)")

        bank = [ctx.enter_context(nc.psum_tensor(f"bank{i}", [P, 512], F32)) for i in range(BANKS)]
        y_ps = [ctx.enter_context(nc.psum_tensor(f"y_ps{i}", [P, 512], F32)) for i in range(2)]

        per_chunk = {
            "rms1": 1, "sqrt1": 1, "x_norm": 1, "rot": 1, "ret_qd": 1, "ret_out_ready": 1, "sqrt_ret": 1,
            "ret_mixed": 1, "conv_done": 3, "silu_conv": 3, "sq": 1, "normed": 1, "sp_in": 1, "exp_ab": 1,
            "ln_ab": 1, "beta_g": 1, "diff": 1, "exp_diff": 1, "small_exp": 1, "kst_scale": 1, "qd": 1,
            "kbe": 1, "T_init": 1, "gdn_ss": 1, "gdn_ms": 1, "sqrt_gdn": 1, "mixed": 1, "rms2": 1,
            "sqrt2": 1, "h2": 1, "gate_in": 1, "gate_exp": 1, "routed": 1,
            "peer_in": 1, "ids_late": 1, "gelu": PH, "weight": PH, "diag": SLOTS, "yss": 1, "yms": 1,
            "sqrt_y": 1, "y_out": 1, "pe_done": 1,
        }
        for _, e, m, _ in USES:
            per_chunk[e] = m
        S = {e: sem(e) for e in per_chunk}
        full = sem("bank_full")
        const_in, x_loaded, y_stored = sem("const_in"), sem("x_loaded"), sem("y_stored")
        start_up = sem("start_up")
        passed = sem("passed")
        w_loaded = [sem(f"w_loaded{i}") for i in range(2)]
        w_free = sem("w_free")
        u_loaded = [sem(f"u_loaded{i}") for i in range(RING)]
        v_loaded = [sem(f"v_loaded{i}") for i in range(RING)]
        u_used, v_used = sem("u_used"), sem("v_used")
        mix_chain, peer_chain = sem("mix_chain"), sem("peer_chain")
        N_CONST = 11

        def event(name, n, i=0):
            return S[name], n * per_chunk[name] + i + 1

        def event_before(name, n):
            return S[name], n * per_chunk[name]

        def used(sem_, n, s):
            return sem_, n * SLOTS + (s + 1 + COUNT0)

        def filled(eng, name, n):
            eng.wait_ge(full, n * len(USES) + PLACE[name] + 1)
            return bank[PLACE[name] % BANKS]

        def follows(eng, name, n):
            if not isinstance(n, int) or n > 0:
                eng.wait_ge(*event_before(name, n))

        block = ctx.enter_context(nc.Block())

        @block.sync
        def _(sp):
            for dst, src in ((tab[:, :, :], tables), (ropes[:, :, :, :], rope), (ret_qdec[:, :, :], qdec),
                             (smalls[:, :], small), (lnT[:, :], cols[:, 0:KT]),
                             (conv_w[:, :, :], cols[:, KT:].rearrange("p (c j) -> p c j", j=4)),
                             (w_ab_sb[:, :, :], w_ab), (keys_sb[:, :, :], keysT),
                             (ln2_row, rows[0].partition_broadcast(P)), (lnf_row, rows[1].partition_broadcast(P)),
                             (headsb[:, :], head_rows.partition_broadcast(P))):
                sp.dma_start(dst, src).then_inc(const_in, 16)
            sp.dma_start(x_in[:, :], x[0]).then_inc(x_loaded, 16)

            def blocks(n):
                with sp.Fori(0, BLOCKS // 2) as b:
                    for i in range(2):
                        sp.wait_ge(w_free, n * BLOCKS + b * 2 + (i + 1))
                        sp.dma_start(wbuf[i][:, :, :], w[bass.ds(b * 2 + i, 1)].rearrange("o p k c -> (o p) k c")
                                     ).then_inc(w_loaded[i], 16)

            with sp.Fori(0, NCH - 1) as n:
                blocks(n)
                sp.wait_ge(*event("x2", n, 1))
                sp.dma_start(x_in[:, :], x[bass.ds(n + 1, 1)].rearrange("o p d -> (o p) d")).then_inc(x_loaded, 16)
            blocks(NCH - 1)

        @block.gpsimd
        def _(pool):
            nc.gpsimd.iota(pos[:, 0:TOPK], [[1, TOPK]], base=0, channel_multiplier=0).then_inc(start_up, 1)
            pool.wait_ge(start_up, 1)
            nc.gpsimd.tensor_copy(iota_f[:, :], pos[:, 0:TOPK]).then_inc(start_up, 1)

            def gather(table, row, slot, done):
                nc.gpsimd.indirect_dma_start(
                    out=row, out_offset=None, in_=table,
                    in_offset=bass.IndirectOffsetOnAxis(ap=ids[:, slot:slot + 1], axis=0)).then_inc(done, 16)

            with pool.Fori(0, NCH) as n:
                pool.wait_ge(*event("peer_in", n))
                pool.sem_inc(passed, 1)
                for t in range(TURNS + LAG):
                    for q in range(QUARTER):
                        s = QUARTER * t + q
                        if s == SLOTS - LATE * TOPK:
                            pool.wait_ge(*event("ids_late", n))
                            pool.sem_inc(passed, 1)
                        if s < SLOTS:
                            pool.wait_ge(*used(u_used, n, s - RING))
                            pool.sem_inc(passed, 1)
                            gather(u_tab, urow[s % RING][:, :], s, u_loaded[s % RING])
                        s -= QUARTER * LAG
                        if s >= 0:
                            pool.wait_ge(*used(v_used, n, s - RING))
                            pool.sem_inc(passed, 1)
                            gather(v_tab, vrow[s % RING][:, :], s, v_loaded[s % RING])

        @block.tensor
        def _(pe):
            pe.wait_ge(const_in, 16 * N_CONST)
            mm, tr = nc.tensor.matmul, nc.tensor.transpose

            def peer_turn(n, t):
                if t == LAG:
                    pe.wait_ge(*event("x2", n, 1))
                    pe.wait_ge(S["y_out"], n + 1)
                    for j in range(2):
                        mm(y_ps[j][:, :], ident, x2[:, 512 * j:512 * j + 512], start=True, stop=False,
                           skip_group_check=True)
                for s in range(QUARTER * (t - LAG), QUARTER * (t - LAG + 1)):
                    if s < 0 or s >= SLOTS:
                        continue
                    pe.wait_ge(*event("diag", n, s))
                    pe.wait_ge(v_loaded[s % RING], n * (16 * SLOTS // RING) + 16 * (s // RING + 1))
                    for j in range(2):
                        last = mm(y_ps[j][:, :], diag[:, s % TOPK, :], vrow[s % RING][:, 512 * j:512 * j + 512],
                                  start=False, stop=(s == SLOTS - 1), skip_group_check=True)
                    last.then_inc(v_used, 1)

            def mix(n, turn):
                use = [0]

                def take(name):
                    u = use[0]
                    assert USES[u][0] == name, (USES[u], name)
                    use[0] += 1
                    v = u - BANKS
                    if v >= 0:
                        pe.wait_ge(*event(USES[v][1], n, USES[v][3]))
                    elif not isinstance(n, int) or n > 0:
                        v += NUSE
                        while v >= len(USES):
                            v -= BANKS
                        pe.wait_ge(*event(USES[v][1], n - 1, USES[v][3]))
                    return bank[u % BANKS]

                def given(ins):
                    ins.then_inc(full, 1)

                def transposes(name, src, count):
                    b = take(name)
                    for i in range(count):
                        last = tr(b[:, P * i:P * i + P], src(i), ident)
                    given(last)

                blk = [0]

                def weight_block():
                    i = blk[0]
                    blk[0] += 1
                    pe.wait_ge(w_loaded[i % 2], n * (16 * BLOCKS // 2) + 16 * (i // 2 + 1))
                    return wbuf[i % 2]

                def project_rows(name):
                    b = take(name)
                    for half_ in range(2):
                        wb = weight_block()
                        for k in range(KT):
                            last = mm(b[:, WB * half_:WB * half_ + WB], actT[:, k, :], wb[:, k, :],
                                      start=(k == 0), stop=(k == KT - 1))
                        if half_ == 0:
                            last.then_inc(w_free, 1)
                    given(last)
                    pe.wait_ge(full, n * len(USES) + use[0])
                    pe.sem_inc(w_free, 1)

                def project_cols(name):
                    b = take(name)
                    for half_ in range(2):
                        wb = weight_block()
                        for c in range(2):
                            o = P * (2 * half_ + c)
                            for k in range(KT):
                                last = mm(b[:, o:o + P], wb[:, k, P * c:P * c + P], actT[:, k, :],
                                          start=(k == 0), stop=(k == KT - 1))
                        if half_ == 0:
                            last.then_inc(w_free, 1)
                    given(last)
                    pe.wait_ge(full, n * len(USES) + use[0])
                    pe.sem_inc(w_free, 1)

                def by_head(name, lhs, rhs):
                    b = take(name)
                    for h in range(H):
                        last = mm(b[:, P * h:P * h + P], lhs[:, h, :], rhs[:, h, :], start=True, stop=True)
                    given(last)

                def all_rows(name, rhs):
                    given(mm(take(name)[:, :], ones, rhs.rearrange("p h t -> p (h t)"), start=True, stop=True))

                turn()
                pe.wait_ge(*event("x_norm", n))
                for j in range(2):
                    transposes(f"xT{j}", lambda i: rowbuf[:, P * (4 * j + i):P * (4 * j + i) + P], 4)
                turn()
                pe.wait_ge(*event("hT", n, 1))
                b = take("ab")
                for k in range(KT):
                    last = mm(b[:, 0:2 * H], actT[:, k, :], w_ab_sb[:, k, :], start=(k == 0), stop=(k == KT - 1))
                given(last)
                for name in ("gq", "gk", "gv"):
                    project_cols(name)
                    turn()
                pe.wait_ge(*event("beta_g", n))
                given(mm(take("gc")[:, 0:H], causal, st[:, 20:24], start=True, stop=True))
                all_rows("gc_row", T[:, :, :])
                all_rows("beta_row", TT[:, :, :])
                turn()
                project_rows("rqk")
                turn()
                pe.wait_ge(*event("sq", n))
                all_rows("ssq", norms[:, 0:4, :])
                all_rows("ssk", norms[:, 4:8, :])
                turn()
                project_rows("rv")
                turn()
                pe.wait_ge(*event("normed", n))
                transposes("kT", lambda i: conv[:, 4 + i, :], 4)
                transposes("vT", lambda i: conv[:, 8 + i, :], 4)
                pe.wait_ge(*event("kbT", n))
                by_head("kk", conv[:, 4:8, :], kbT)
                by_head("qk", conv[:, 4:8, :], conv[:, 0:4, :])
                turn()
                project_rows("rg")
                turn()

                def ret_transposes():
                    pe.wait_ge(*event("rot", n))
                    transposes("retT", lambda i: ret_rot[:, 2 * i:2 * i + 2, :, :].rearrange("p a z d -> p (a z d)"), 4)

                def ret_scores():
                    pe.wait_ge(*event("ret_qd", n))
                    b = take("ret_s")
                    for h in range(H):
                        last = mm(b[:, P * h:P * h + P], retT[:, 2 + h // 2, :], ret_qz[:, h, :], start=True, stop=True)
                    given(last)

                def ret_out():
                    pe.wait_ge(*event("ret_s", n))
                    pe.wait_ge(*event("vr_in", n))
                    follows(pe, "ret_state", n)
                    if isinstance(n, int):
                        pe.wait_ge(start_up, 3)
                    b = take("ret_out")
                    for h in range(H):
                        mm(b[:, P * h:P * h + P], ret_s[:, h, :], v_r[:, h, :], start=True, stop=False)
                        last = mm(b[:, P * h:P * h + P], ret_qd[:, h, :], state_r[:, h // 2, :], start=False, stop=True)
                    given(last)
                    b = take("ret_kv")
                    for h in range(H):
                        p0 = 64 * (h % 2)
                        last = mm(b[p0:p0 + 64, P * (h // 2):P * (h // 2) + P], ret_kd[:, h, :], v_r[:, h, :],
                                  start=True, stop=True)
                    given(last)

                between = {0: lambda: project_rows("gz"), 1: ret_transposes, 2: ret_scores, 3: ret_out}

                pe.wait_ge(*event("NT", n))
                pe.wait_ge(*event("T_init", n))
                for i in range(LEVELS):
                    if i:
                        pe.wait_ge(*event("inv_TT", n, i - 1))
                    by_head(f"P{i}", NT, T)
                    if i in between:
                        between[i]()
                    turn()
                    pe.wait_ge(*event("inv_P", n, i))
                    by_head(f"Q{i}", TT, Pm)
                    by_head(f"R{i}", Pm, TT)
                    turn()
                pe.wait_ge(*event("inv_TT", n, LEVELS - 1))
                pe.wait_ge(*event("kbe", n))
                by_head("wT", kbe, TT)
                turn()
                pe.wait_ge(*event("wT", n))
                follows(pe, "gdn_state", n)
                b = take("vnew")
                for h in range(H):
                    mm(b[:, P * h:P * h + P], TT[:, h, :], vb[:, h, :], start=True, stop=False)
                    last = mm(b[:, P * h:P * h + P], wT[:, h, :], state_g[:, h, :], start=False, stop=True)
                given(last)
                turn()
                pe.wait_ge(*event("vnew", n))
                pe.wait_ge(*event("qd", n))
                b = take("gdn_out")
                for h in range(H):
                    mm(b[:, P * h:P * h + P], qdT[:, h, :], state_g[:, h, :], start=True, stop=False)
                    last = mm(b[:, P * h:P * h + P], attnT[:, h, :], vnew[:, h, :], start=False, stop=True)
                given(last)
                by_head("gdn_kv", kst, vnew)
                turn()
                pe.wait_ge(*event("mixed", n))
                pe.wait_ge(*event("ret_mixed", n))
                for j in range(2):
                    transposes(f"mT{j}", lambda i: rowbuf[:, P * (4 * j + i):P * (4 * j + i) + P], 4)
                turn()
                pe.wait_ge(*event("mT", n, 1))
                for j in range(2):
                    project_rows(f"out{j}")
                    turn()
                pe.wait_ge(*event("h2", n))
                for j in range(2):
                    transposes(f"h2T{j}", lambda i: rowbuf[:, P * (4 * j + i):P * (4 * j + i) + P], 4)
                turn()
                pe.wait_ge(*event("h2T", n, 1))
                for j in range(4):
                    project_cols(f"q{j}")
                    turn()
                for j in range(4):
                    pe.wait_ge(*event("qT", n, j))
                    b = take(f"s{j}")
                    for i in range(4):
                        last = mm(b[:, P * i:P * i + P], qT[:, 4 * j + i, :], keys_sb[:, 4 * j + i, :],
                                  start=True, stop=True)
                    given(last)
                for _ in range(8):
                    turn()
                assert use[0] == len(USES) and blk[0] == BLOCKS

            pe.sem_inc(w_free, 2)
            pe.sem_inc(v_used, COUNT0)
            chunks(pe, mix, peer_turn, lambda n: None)

        @block.scalar
        def _(act):
            act.wait_ge(const_in, 16 * N_CONST)
            act.wait_ge(start_up, 3)
            A = nc.scalar.activation
            A(neg_a[:, :], a_log, ACT.Exp).then_inc(start_up, 1)

            def peer_turn(n, t):
                if t % QUARTER == 0 and 0 < t <= TURNS:
                    h = t // QUARTER - 1
                    act.wait_ge(*used(u_used, n, TOPK * h + TOPK - 1))
                    A(gelu[:, TOPK * h:TOPK * h + TOPK], dots[:, TOPK * h:TOPK * h + TOPK], ACT.Gelu
                      ).then_inc(S["gelu"], 1)
                if t % QUARTER == 1 and 1 < t <= TURNS + 1:
                    h = t // QUARTER - 1
                    act.wait_ge(*event("weight", n, h))
                    for k in range(TOPK):
                        s = TOPK * h + k
                        act.wait_ge(*used(v_used, n, s - TOPK))
                        A(diag[:, k, :], ident, ACT.Copy, scale=weight[:, s:s + 1]).then_inc(S["diag"], 1)

            def finish(n):
                act.wait_ge(*used(v_used, n, SLOTS - 1))
                A(y_sb[:, 0:512], y_ps[0][:, :], ACT.Square, accum_out=st[:, 60:61])
                A(y_sb[:, 512:1024], y_ps[1][:, :], ACT.Square, accum_out=st[:, 61:62]).then_inc(S["yss"], 1)
                act.wait_ge(*event("yms", n))
                A(st[:, 59:60], st[:, 58:59], ACT.Sqrt).then_inc(S["sqrt_y"], 1)
                act.wait_ge(S["y_out"], n + 2)
                act.dma_start(out[at(n)].rearrange("o p d -> (o p) d"), y_sb[:, :]).then_inc(y_stored, 16)
                act.wait_ge(y_stored, n * 16 + 16)

            def mix(n, turn):
                def heads(ap):
                    return ap[:, :].rearrange("p (h t) -> p h t", t=P)

                def put(name, use, dst, f=ACT.Copy, **kw):
                    A(dst, heads(filled(act, use, n)), f, **kw).then_inc(S[name], 1)

                def conv_silu(j):
                    act.wait_ge(*event("conv_done", n, j))
                    A(conv[:, 4 * j:4 * j + 4, :], conv[:, 4 * j:4 * j + 4, :], ACT.Silu).then_inc(S["silu_conv"], 1)

                turn()
                act.wait_ge(*event("rms1", n))
                A(st[:, 1:2], st[:, 0:1], ACT.Sqrt).then_inc(S["sqrt1"], 1)
                turn()
                act.wait_ge(*event("sp_in", n))
                A(st[:, 8:12], st[:, 4:8], ACT.Exp)
                A(st[:, 12:16], ab[:, 1, :], ACT.Exp, scale=-1.0).then_inc(S["exp_ab"], 1)
                act.wait_ge(*event("exp_ab", n))
                A(st[:, 16:20], st[:, 8:12], ACT.Ln, bias=1.0).then_inc(S["ln_ab"], 1)
                follows(act, "conv_done", n)
                for j, use in enumerate(("gq", "gk", "gv")):
                    put("conv_in", use, conv_in[:, 4 * j:4 * j + 4, 3:P + 3])
                    if j:
                        conv_silu(j - 1)
                    turn()
                act.wait_ge(*event("diff", n))
                A(cmask[:, :, :], cmask[:, :, :], ACT.Exp)
                A(st[:, 36:44], st[:, 44:52], ACT.Exp).then_inc(S["exp_diff"], 1)
                put("E", "gc_row", expg[:, :, :], ACT.Exp)
                turn()
                conv_silu(2)
                act.wait_ge(*event("silu_conv", n, 1))
                A(norms[:, :, :], conv[:, 0:8, :], ACT.Square).then_inc(S["sq"], 1)
                follows(act, "ret_qd", n)
                put("qk_in", "rqk", qk_r[:, :, :, :].rearrange("p (a h) z d -> p a (h z d)", a=4))
                turn()
                put("norm_in", "ssq", norms[:, 0:4, :], ACT.Sqrt, bias=eps_col[:, 0:1])
                put("norm_in", "ssk", norms[:, 4:8, :], ACT.Sqrt, bias=eps_col[:, 0:1])
                turn()
                follows(act, "ret_state", n)
                put("vr_in", "rv", v_r[:, :, :])
                turn()
                turn()
                follows(act, "ret_mixed", n)
                put("gR_in", "rg", gate_r[:, :, :], ACT.Silu)
                turn()
                for i in range(LEVELS):
                    if i == 0:
                        follows(act, "mixed", n)
                        put("gG_in", "gz", gate_g[:, :, :], ACT.Silu)
                    if i == 1:
                        put("retT", "retT", retT[:, :, :])
                    turn()
                    if i == 3:
                        act.wait_ge(*event("ret_out_ready", n))
                        A(st[:, 28:32], mv[:, :, 1], ACT.Sqrt, bias=eps_col[:, 0:1]).then_inc(S["sqrt_ret"], 1)
                    turn()
                put("wT", "wT", wT[:, :, :], scale=-1.0)
                turn()
                put("vnew", "vnew", vnew[:, :, :])
                turn()
                b = filled(act, "gdn_out", n)
                for h in range(H):
                    last = A(qdT[:, h, :], b[:, P * h:P * h + P], ACT.Square, accum_out=st[:, 52 + h:53 + h])
                last.then_inc(S["gdn_ss"], 1)
                act.wait_ge(*event("gdn_ms", n))
                A(st[:, 32:36], st[:, 24:28], ACT.Sqrt).then_inc(S["sqrt_gdn"], 1)
                turn()
                for j in range(2):
                    put("mT", f"mT{j}", actT[:, 4 * j:4 * j + 4, :])
                turn()
                turn()
                turn()
                act.wait_ge(*event("rms2", n))
                A(st[:, 1:2], st[:, 0:1], ACT.Sqrt).then_inc(S["sqrt2"], 1)
                for j in range(2):
                    put("h2T", f"h2T{j}", actT[:, 4 * j:4 * j + 4, :])
                turn()
                for j in range(4):
                    put("qT", f"q{j}", qT[:, 4 * j:4 * j + 4, :])
                    turn()
                for j in range(4):
                    put("scores", f"s{j}", scores[:, 4 * j:4 * j + 4, :])
                for _ in range(5):
                    turn()
                act.wait_ge(*event("gate_in", n))
                A(best[:, :, :], best[:, :, :], ACT.Exp).then_inc(S["gate_exp"], 1)
                for _ in range(3):
                    turn()

            chunks(act, mix, peer_turn, finish)

        @block.vector
        def _(dve):
            V = nc.vector
            MIX_LINKS, PEER_LINKS = 50, 3
            V.memset(state_g[:, :, :], 0.0)
            V.memset(state_r[:, :, :], 0.0)
            V.memset(conv_in[:, :, 0:3], 0.0)
            dve.wait_ge(start_up, 2)
            V.memset(eps_col[:, :], EPS).then_inc(start_up, 1)
            dve.wait_ge(start_up, 4)
            V.tensor_scalar(neg_a[:, :], neg_a[:, :], -1.0, None, ALU.mult).then_inc(start_up, 1)
            dve.wait_ge(start_up, 5)
            dve.wait_ge(const_in, 16 * N_CONST)
            dve.sem_inc(u_used, COUNT0)
            dve.sem_inc(S["y_out"], 1)

            def peer_turn(n, t):
                if t == 0:
                    dve.wait_ge(*used(u_used, n, -1))
                    follows(dve, "weight", n)
                    V.tensor_copy(h2[:, :], rowbuf[:, :])
                    V.tensor_copy(gate[:, :], gate_next[:, :])
                    dve.wait_ge(*used(v_used, n, -LATE * TOPK - 1))
                    V.tensor_copy(ids[:, 0:SLOTS - LATE * TOPK], ids_next[:, 0:SLOTS - LATE * TOPK]
                                  ).then_inc(S["peer_in"], 1)
                    dve.wait_ge(*event("peer_in", n))
                if t == LAG:
                    dve.wait_ge(*used(v_used, n, -1))
                    V.tensor_copy(ids[:, SLOTS - LATE * TOPK:], ids_next[:, SLOTS - LATE * TOPK:]
                                  ).then_inc(S["ids_late"], 1)
                if t < TURNS:
                    for s in range(QUARTER * t, QUARTER * t + QUARTER):
                        u = urow[s % RING][:, :]
                        dve.wait_ge(u_loaded[s % RING], n * (16 * SLOTS // RING) + 16 * (s // RING + 1))
                        V.tensor_tensor_reduce(out=u, in0=u, in1=h2[:, :], scale=1.0, scalar=0.0, op0=ALU.mult,
                                               op1=ALU.add, accum_out=dots[:, s:s + 1]).then_inc(u_used, 1)
                if t % QUARTER == 0 and 0 < t <= TURNS:
                    h = t // QUARTER - 1
                    c0, c1 = TOPK * h, TOPK * h + TOPK
                    dve.wait_ge(*event("gelu", n, h))
                    V.tensor_tensor(weight[:, c0:c1], gelu[:, c0:c1], gate[:, c0:c1], ALU.mult).then_inc(S["weight"], 1)

            def finish(n):
                base = n * PEER_LINKS
                dve.wait_ge(*event("yss", n))
                V.tensor_tensor(st[:, 57:58], st[:, 60:61], st[:, 61:62], ALU.add).then_inc(peer_chain, 1)
                dve.wait_ge(peer_chain, base + 1)
                V.tensor_scalar(st[:, 58:59], st[:, 57:58], 1.0 / D, EPS, ALU.mult, ALU.add).then_inc(S["yms"], 1)
                dve.wait_ge(*event("sqrt_y", n))
                V.reciprocal(st[:, 57:58], st[:, 59:60]).then_inc(peer_chain, 1)
                dve.wait_ge(peer_chain, base + 2)
                V.scalar_tensor_tensor(y_sb[:, 0:512], y_ps[0][:, :], st[:, 57:58], lnf_row[:, 0:512],
                                       ALU.mult, ALU.mult).then_inc(peer_chain, 1)
                V.scalar_tensor_tensor(y_sb[:, 512:1024], y_ps[1][:, :], st[:, 57:58], lnf_row[:, 512:1024],
                                       ALU.mult, ALU.mult).then_inc(S["y_out"], 1)

            def mix(n, turn):
                links = [0]

                def link(ins, apart=False):
                    links[0] += 1
                    ins.then_inc(mix_chain, 1)
                    dve.wait_ge(mix_chain, n * MIX_LINKS + links[0])
                    if apart:
                        dve.sem_inc(passed, 1)

                def heads(ap):
                    return ap[:, :].rearrange("p (h t) -> p h t", t=P)

                def by_head(ap, k=P):
                    return ap.unsqueeze(2).broadcast_to([P, ap.shape[1], k])

                def each_head(ap):
                    return ap.unsqueeze(1).broadcast_to([P, H, P])

                turn()
                dve.wait_ge(x_loaded, n * 16 + 16)
                link(V.tensor_tensor_reduce(out=rowbuf[:, :], in0=x_in[:, :], in1=x_in[:, :], scale=1.0, scalar=0.0,
                                            op0=ALU.mult, op1=ALU.add, accum_out=st[:, 2:3]))
                V.tensor_scalar(st[:, 0:1], st[:, 2:3], 1.0 / D, EPS, ALU.mult, ALU.add).then_inc(S["rms1"], 1)
                dve.wait_ge(*event("sqrt1", n))
                link(V.reciprocal(st[:, 2:3], st[:, 1:2]))
                V.tensor_scalar(rowbuf[:, :], x_in[:, :], st[:, 2:3], None, ALU.mult).then_inc(S["x_norm"], 1)
                turn()
                for j in range(2):
                    V.tensor_tensor(actT[:, 4 * j:4 * j + 4, :], heads(filled(dve, f"xT{j}", n)),
                                    by_head(lnT[:, 4 * j:4 * j + 4]), ALU.mult).then_inc(S["hT"], 1)
                link(V.tensor_copy(ab[:, :, :].rearrange("p a h -> p (a h)"), filled(dve, "ab", n)[:, 0:2 * H]))
                V.tensor_copy(st[:, 3:4], ab[:, 0, 0:1]).then_inc(S["ab_in"], 1)
                link(V.tensor_tensor(st[:, 52:56], ab[:, 0, :], dt_bias, ALU.add))
                link(V.tensor_scalar(st[:, 4:8], st[:, 52:56], -1.0, None, ALU.mult))
                V.tensor_tensor(st[:, 4:8], st[:, 4:8], st[:, 52:56], ALU.min).then_inc(S["sp_in"], 1)

                def convolve(part):
                    dve.wait_ge(*event("conv_in", n, part))
                    for j in range(4):
                        for c in range(4 * part, 4 * part + 4):
                            src = conv_in[:, c, j:j + P]
                            if j == 0:
                                last = V.tensor_scalar(conv[:, c, :], src, conv_w[:, c, 0:1], None, ALU.mult)
                            else:
                                last = V.scalar_tensor_tensor(conv[:, c, :], src, conv_w[:, c, j:j + 1],
                                                              conv[:, c, :], ALU.mult, ALU.add)
                        link(last)
                    tiles = conv_in[:, 4 * part:4 * part + 4, :]
                    V.tensor_copy(tiles[:, :, 0:3], tiles[:, :, P:P + 3]).then_inc(S["conv_done"], 1)

                convolve(0)
                turn()
                dve.wait_ge(*event("ln_ab", n))
                link(V.tensor_scalar(st[:, 4:8], st[:, 52:56], 0.0, None, ALU.max))
                V.tensor_scalar(st[:, 12:16], st[:, 12:16], 1.0, None, ALU.add)
                link(V.tensor_tensor(st[:, 4:8], st[:, 4:8], st[:, 16:20], ALU.add))
                V.tensor_tensor(st[:, 20:24], st[:, 4:8], neg_a[:, :], ALU.mult)
                link(V.reciprocal(st[:, 24:28], st[:, 12:16]))
                V.tensor_tensor(T[:, :, :], each_head(causal), by_head(st[:, 20:24]), ALU.mult)
                V.tensor_tensor(TT[:, :, :], each_head(ident), by_head(st[:, 24:28]), ALU.mult).then_inc(S["beta_g"], 1)
                convolve(1)
                turn()
                convolve(2)
                turn()
                link(V.tensor_copy(st[:, 44:48], filled(dve, "gc", n)[:, 0:H]))
                V.tensor_copy(st[:, 3:4], st[:, 44:45]).then_inc(S["gc_in"], 1)
                b = filled(dve, "gc_row", n)
                for h in range(H):
                    V.tensor_scalar(cmask[:, h, :], b[:, P * h:P * h + P], st[:, 44 + h:45 + h], 0.0,
                                    ALU.subtract, ALU.min)
                V.tensor_tensor(st[:, 48:52], heads(b)[:, :, P - 1], st[:, 44:48], ALU.subtract).then_inc(S["diff"], 1)
                turn()
                dve.wait_ge(*event("exp_diff", n))
                V.tensor_tensor(st[:, 36:40], st[:, 36:40], st[:, 24:28], ALU.mult)
                link(V.tensor_tensor(cmask[:, :, :], cmask[:, :, :], each_head(causal), ALU.mult))
                turn()
                turn()
                dve.wait_ge(*event("norm_in", n, 1))
                link(V.reciprocal(norms[:, :, :], norms[:, :, :]))
                V.scalar_tensor_tensor(conv[:, 0:4, :].rearrange("p h t -> p (h t)"),
                                       conv[:, 0:4, :].rearrange("p h t -> p (h t)"), float(DV) ** -0.5,
                                       norms[:, 0:4, :].rearrange("p h t -> p (h t)"), ALU.mult, ALU.mult)
                V.tensor_tensor(conv[:, 4:8, :], conv[:, 4:8, :], norms[:, 4:8, :], ALU.mult).then_inc(S["normed"], 1)
                dve.wait_ge(*event("normed", n))
                V.tensor_tensor(kbT[:, :, :], conv[:, 4:8, :], heads(filled(dve, "beta_row", n)), ALU.mult
                                ).then_inc(S["kbT"], 1)
                V.tensor_copy(T[:, :, :], each_head(ident))
                V.tensor_copy(TT[:, :, :], each_head(ident)).then_inc(S["T_init"], 1)
                dve.wait_ge(*event("E", n))
                V.tensor_tensor(qdT[:, :, :], conv[:, 0:4, :], expg[:, :, :], ALU.mult).then_inc(S["qd"], 1)
                turn()
                b = filled(dve, "kT", n)
                V.tensor_tensor(kbe[:, :, :], heads(b), by_head(st[:, 36:40]), ALU.mult).then_inc(S["kbe"], 1)
                V.tensor_tensor(kst[:, :, :], heads(b), by_head(st[:, 40:44]), ALU.mult).then_inc(S["kst"], 1)
                V.tensor_tensor(vb[:, :, :], heads(filled(dve, "vT", n)), by_head(st[:, 24:28]), ALU.mult
                                ).then_inc(S["vb"], 1)
                link(V.tensor_tensor(NT[:, :, :], heads(filled(dve, "kk", n)), cmask[:, :, :], ALU.mult))
                V.tensor_tensor(NT[:, :, :], NT[:, :, :], each_head(strict), ALU.mult).then_inc(S["NT"], 1)
                V.tensor_tensor(attnT[:, :, :], heads(filled(dve, "qk", n)), cmask[:, :, :], ALU.mult
                                ).then_inc(S["attn"], 1)
                turn()
                dve.wait_ge(*event("qk_in", n))
                q1, q2 = qk_r[:, :, 0, :], qk_r[:, :, 1, :]
                cos, sin, nsin = (ropes[:, i, at(n), :].broadcast_to([P, 2 * H, 32]) for i in range(3))
                V.tensor_tensor(ret_rot[:, :, 0, :], q1, cos, ALU.mult)
                V.tensor_tensor(ret_rot[:, :, 1, :], q2, cos, ALU.mult)
                V.tensor_tensor(ret_tmp[:, :, 0, :], q2, nsin, ALU.mult)
                link(V.tensor_tensor(ret_tmp[:, :, 1, :], q1, sin, ALU.mult))
                V.tensor_tensor(ret_rot[:, :, :, :], ret_rot[:, :, :, :], ret_tmp[:, :, :, :], ALU.add
                                ).then_inc(S["rot"], 1)
                dve.wait_ge(*event("rot", n))
                V.tensor_tensor(ret_kd[:, :, :], ret_rot[:, H:2 * H, :, :].rearrange("p h z d -> p h (z d)"),
                                by_head(smalls[:, 0:4], 64), ALU.mult)
                turn()

                def ret_queries():
                    dve.wait_ge(*event("retT", n))
                    for h in range(H):
                        V.tensor_scalar(ret_qz[:, h, :], retT[:, h // 2, :], smalls[:, 6 + h:7 + h], None, ALU.mult)
                        last = V.tensor_tensor(ret_qd[:, h, :], retT[:, h // 2, :], ret_qdec[:, h, :], ALU.mult)
                    last.then_inc(S["ret_qd"], 1)

                def ret_decay_scores():
                    V.tensor_tensor(ret_s[:, :, :], heads(filled(dve, "ret_s", n)), ret_decay, ALU.mult
                                    ).then_inc(S["ret_s"], 1)

                def ret_moments():
                    b = filled(dve, "ret_kv", n)
                    for j in range(2):
                        last = V.scalar_tensor_tensor(state_r[:, j, :], state_r[:, j, :], smalls[:, 4 + j:5 + j],
                                                      b[:, P * j:P * j + P], ALU.mult, ALU.add)
                    last.then_inc(S["ret_state"], 1)
                    b = filled(dve, "ret_out", n)
                    for h in range(H):
                        last = V.bn_stats(bn[:, h, :], b[:, P * h:P * h + P])
                    link(last, apart=True)
                    for h in range(H):
                        last = V.bn_aggr(mv[:, h, :], bn[:, h, :])
                    last.then_inc(S["ret_out_ready"], 1)
                    V.tensor_tensor(gate_r[:, :, :].rearrange("p h d -> p (h d)"),
                                    gate_r[:, :, :].rearrange("p h d -> p (h d)"), retw_row, ALU.mult)

                def ret_group_norm():
                    dve.wait_ge(*event("sqrt_ret", n))
                    b = filled(dve, "ret_out", n)
                    link(V.reciprocal(st[:, 32:36], st[:, 28:32]))
                    for h in range(H):
                        last = V.tensor_scalar(ret_s[:, h, :], b[:, P * h:P * h + P], mv[:, h, 0:1],
                                               st[:, 32 + h:33 + h], ALU.subtract, ALU.mult)
                    last.then_inc(S["ret_norm"], 1)
                    dve.wait_ge(*event("ret_norm", n))
                    V.tensor_tensor(rowbuf[:, 0:512], ret_s[:, :, :].rearrange("p h d -> p (h d)"),
                                    gate_r[:, :, :].rearrange("p h d -> p (h d)"), ALU.mult).then_inc(S["ret_mixed"], 1)

                def gate_weight():
                    dve.wait_ge(*event("gG_in", n))
                    V.tensor_tensor(gate_g[:, :, :], gate_g[:, :, :], each_head(gdnw_row), ALU.mult)

                between = {1: ret_queries, 2: ret_decay_scores, 3: ret_moments, 4: ret_group_norm, 5: gate_weight}
                for i in range(LEVELS):
                    V.tensor_tensor(Pm[:, :, :], heads(filled(dve, f"P{i}", n)), each_head(level_mask[i]), ALU.mult
                                    ).then_inc(S["inv_P"], 1)
                    if i in between:
                        between[i]()
                    turn()
                    b2 = filled(dve, f"R{i}", n)
                    b = bank[PLACE[f"Q{i}"] % BANKS]
                    V.tensor_tensor(T[:, :, :], T[:, :, :], heads(b), ALU.subtract).then_inc(S["inv_T"], 1)
                    V.tensor_tensor(TT[:, :, :], TT[:, :, :], heads(b2), ALU.subtract).then_inc(S["inv_TT"], 1)
                    turn()
                turn()
                turn()
                b = filled(dve, "gdn_out", n)
                dve.wait_ge(*event("gdn_ss", n))
                V.tensor_scalar(st[:, 24:28], st[:, 52:56], 1.0 / DV, EPS, ALU.mult, ALU.add).then_inc(S["gdn_ms"], 1)
                b2 = filled(dve, "gdn_kv", n)
                for h in range(H):
                    last = V.scalar_tensor_tensor(state_g[:, h, :], state_g[:, h, :], expg[:, h, P - 1:P],
                                                  b2[:, P * h:P * h + P], ALU.mult, ALU.add)
                last.then_inc(S["gdn_state"], 1)
                dve.wait_ge(*event("sqrt_gdn", n))
                link(V.reciprocal(st[:, 28:32], st[:, 32:36]))
                for h in range(H):
                    last = V.scalar_tensor_tensor(rowbuf[:, 512 + P * h:512 + P * h + P], b[:, P * h:P * h + P],
                                                  st[:, 28 + h:29 + h], gate_g[:, h, :], ALU.mult, ALU.mult)
                last.then_inc(S["gdn_norm"], 1)
                V.tensor_copy(st[:, 3:4], st[:, 28:29]).then_inc(S["mixed"], 1)
                turn()
                turn()
                for j in range(2):
                    b = filled(dve, f"out{j}", n)
                    if j == 0 and (not isinstance(n, int) or n > 0):
                        dve.wait_ge(*used(v_used, n - 1, 0))
                    V.tensor_tensor(x2[:, 512 * j:512 * j + 512], b[:, :], x_in[:, 512 * j:512 * j + 512], ALU.add
                                    ).then_inc(S["x2"], 1)
                    turn()
                dve.wait_ge(*event("x2", n, 1))
                link(V.tensor_tensor_reduce(out=rowbuf[:, :], in0=x2[:, :], in1=x2[:, :], scale=1.0, scalar=0.0,
                                            op0=ALU.mult, op1=ALU.add, accum_out=st[:, 2:3]))
                V.tensor_scalar(st[:, 0:1], st[:, 2:3], 1.0 / D, EPS, ALU.mult, ALU.add).then_inc(S["rms2"], 1)
                dve.wait_ge(*event("sqrt2", n))
                link(V.reciprocal(st[:, 2:3], st[:, 1:2]))
                V.scalar_tensor_tensor(rowbuf[:, :], x2[:, :], st[:, 2:3], ln2_row, ALU.mult, ALU.mult
                                       ).then_inc(S["h2"], 1)
                turn()
                for j in range(4):
                    turn()
                dve.wait_ge(*event("scores", n, 3))
                dve.sem_inc(passed, 1)

                def top16(count, src, vals, index):
                    for part in range(2):
                        o = 8 * part
                        for t in range(count):
                            last = V.max(vals(t)[:, o:o + 8], src(t))
                        link(last, apart=True)
                        for t in range(count):
                            last = V.max_index(index(t)[:, o:o + 8], vals(t)[:, o:o + 8], src(t))
                        if part == 0:
                            for t in range(count):
                                last = V.match_replace(src(t), vals(t)[:, 0:8], src(t), LOWEST)
                        link(last, apart=True)
                        turn()

                top16(16, lambda t: scores[:, t, :], lambda t: top_v[:, t, :], lambda t: top_i[:, t, :])
                turn()
                V.tensor_copy(top_if[:, :, :], top_i[:, :, :])
                for h in range(PH):
                    last = V.tensor_tensor(
                        cand[:, h, :].rearrange("p (a b) -> p a b", b=TOPK),
                        top_v[:, 2 * h, :].unsqueeze(2).broadcast_to([P, TOPK, TOPK]),
                        top_v[:, 2 * h + 1, :].unsqueeze(1).broadcast_to([P, TOPK, TOPK]), ALU.add)
                link(last, apart=True)
                top16(PH, lambda t: cand[:, t, :], lambda t: best[:, t, :], lambda t: pos[:, TOPK * t:TOPK * t + TOPK])
                V.tensor_scalar(pos2[:, 0, :], pos[:, :], 4, None, ALU.logical_shift_right)
                link(V.tensor_scalar(pos2[:, 1, :], pos[:, :], TOPK - 1, None, ALU.bitwise_and))
                link(V.tensor_copy(pos_f[:, :, :], pos2[:, :, :]))
                link(V.tensor_copy(st[:, 52:60], best[:, :, 0]))
                V.tensor_tensor(best[:, :, :], best[:, :, :], by_head(st[:, 52:60], TOPK), ALU.subtract
                                ).then_inc(S["gate_in"], 1)
                iota_all = iota_f[:, :].unsqueeze(1).broadcast_to([P, SLOTS, TOPK])
                for z in range(2):
                    link(V.tensor_tensor(picked[:, :, :], by_head(pos_f[:, z, :], TOPK), iota_all, ALU.is_equal))
                    for h in range(PH):
                        last = V.tensor_tensor(picked[:, TOPK * h:TOPK * h + TOPK, :], picked[:, TOPK * h:TOPK * h + TOPK, :],
                                               top_if[:, 2 * h + z, :].unsqueeze(1).broadcast_to([P, TOPK, TOPK]), ALU.mult)
                    link(last)
                    link(V.tensor_reduce(sel[:, z, :], picked[:, :, :], AX, ALU.add))
                    turn()
                V.scalar_tensor_tensor(ids_next[:, :], sel[:, 0, :], float(KEYS), sel[:, 1, :], ALU.mult, ALU.add)
                dve.wait_ge(*event("gate_exp", n))
                link(V.tensor_reduce(st[:, 52:60], best[:, :, :], AX, ALU.add))
                link(V.reciprocal(st[:, 52:60], st[:, 52:60]))
                V.tensor_tensor(gate_next[:, :].rearrange("p (h k) -> p h k", k=TOPK), best[:, :, :],
                                by_head(st[:, 52:60], TOPK), ALU.mult).then_inc(S["routed"], 1)
                turn()
                dve.wait_ge(*event("routed", n))
                assert links[0] == MIX_LINKS, links

            chunks(dve, mix, peer_turn, finish)


def at(n):
    return slice(n, n + 1) if isinstance(n, int) else bass.ds(n, 1)


def chunks(eng, mix, peer_turn, finish):
    def together(n, first=False, mixing=True):
        t, mark = [0], [0]

        def turn():
            mark[0] += 1
            for _ in range(PACE[mark[0] - 1]):
                one()

        def one():
            if t[0] < TURNS + LAG:
                if t[0] == LAG - 1 and not first:
                    finish(n - 1)
                peer_turn(n, t[0])
                t[0] += 1

        if mixing:
            mix(n + 1, turn)
            assert mark[0] == len(PACE), mark
        while t[0] < TURNS + LAG:
            one()

    mix(0, lambda: None)
    together(0, first=True)
    with eng.Fori(1, NCH - 1) as n:
        together(n)
    together(NCH - 1, mixing=False)
    finish(NCH - 1)


def shape_tables():
    i = np.arange(P)
    tables = np.zeros((P, TAB, P), np.float32)
    tables[:, 0] = np.eye(P)
    tables[:, 1] = i[:, None] <= i[None, :]
    tables[:, 2] = i[:, None] < i[None, :]
    tables[:, 3] = 1.0
    for l in range(LEVELS):
        r, c = i[:, None] >> l, i[None, :] >> l
        tables[:, 4 + l] = (r % 2 == 1) & (c == r - 1)
    lg = np.log1p(-np.exp2(-5.0 - np.arange(H)))
    diff = (i[None, :] - i[:, None]).astype(np.float64)
    for h in range(H):
        tables[:, 4 + LEVELS + h] = np.where(diff >= 0, np.exp(lg[h] * np.maximum(diff, 0)), 0) * 64 ** -0.5
    inv = np.float32(10000.0) ** (-np.arange(32, dtype=np.float32) / np.float32(32))
    ang = (np.arange(SEQ, dtype=np.float32)[:, None] * inv[None, :].astype(np.float32)).reshape(NCH, P, 32)
    ang = ang.transpose(1, 0, 2).astype(np.float64)
    rope = np.stack([np.cos(ang), np.sin(ang), -np.sin(ang)], 1).astype(np.float32)
    of = np.array([[2 * j + p // 64 for j in range(2)] for p in range(P)])
    here = (np.arange(H)[None, :] % 2 == i[:, None] // 64).astype(np.float64)
    qdec = (np.exp(lg[:, None] * (i + 1.0)[None, :])[None] * here[:, :, None]).astype(np.float32)
    small = np.concatenate([np.exp(lg[None, :] * (P - 1.0 - i)[:, None]) * 64 ** -0.5, np.exp(lg[of] * P), here], 1)
    return tables, rope, qdec, np.ascontiguousarray(small, np.float32)


def kernel(**inputs):
    import concourse.bacc as bacc
    from concourse.bass_utils import run_bass_kernel_spmd

    a = {k: np.asarray(v) for k, v in inputs.items()}

    def tiles(m, block):
        return m.reshape(KT, P, -1, block).transpose(2, 1, 0, 3)

    w_in = a["w_in"][0]
    by_use = np.r_[6:12, 0:6, 12:14]
    w = np.concatenate([tiles(w_in[:, 0:IN_BLOCKS * WB], WB)[by_use], tiles(a["w_out"][0], WB), tiles(a["peer_wq"][0], WB)])
    w_ab = tiles(w_in[:, IN_BLOCKS * WB:], 2 * H)[0]
    cols = np.concatenate([a["ln1_w"][0].reshape(KT, P).T,
                           a["conv_w"][0].reshape(4, 12, P).transpose(2, 1, 0).reshape(P, 48)], 1)
    head_rows = np.concatenate([a["ret_norm_w"][0], a["gdn_norm_w"][0], a["A_log"][0], a["dt_bias"][0]])
    tables, rope, qdec, small = shape_tables()
    arrays = {
        "x": a["x"].reshape(NCH, P, D), "w": w, "w_ab": w_ab,
        "keysT": a["peer_keys"][0].reshape(16, KEYS, P).transpose(2, 0, 1),
        "u_tab": a["peer_u"][0], "v_tab": a["peer_v"][0], "cols": cols,
        "rows": np.stack([a["ln2_w"][0], a["lnf_w"]]), "head_rows": head_rows,
        "tables": tables, "rope": rope, "qdec": qdec, "small": small,
    }
    nc = bacc.Bacc("TRN2", target_bir_lowering=False, num_devices=1)
    arrays = {k: np.ascontiguousarray(v) for k, v in arrays.items()}
    args = [nc.dram_tensor(k, v.shape, mybir.dt.from_np(v.dtype), kind="ExternalInput").ap() for k, v in arrays.items()]
    args.append(nc.dram_tensor("y", (NCH, P, D), F32, kind="ExternalOutput").ap())
    build(nc, *args)
    r = run_bass_kernel_spmd(nc, [arrays], core_ids=[0])
    return r.results[0]["y"].reshape(1, SEQ, D)
```

```python
from contextlib import ExitStack

import concourse.bass as bass
import numpy as np
from concourse import mybir

ALU = mybir.AluOpType
ACT = mybir.ActivationFunctionType
AX = mybir.AxisListType.X
F32 = mybir.dt.float32
U32 = mybir.dt.uint32

P = 128
D = 1024
KT = D // P
SEQ = 1024
NCH = SEQ // P
H = 4
DV = 128
EPS = 1e-6
WB = 256
IN_BLOCKS, OUT_BLOCKS, Q_BLOCKS = 14, 4, 8
BLOCKS = IN_BLOCKS + OUT_BLOCKS + Q_BLOCKS
NBLOCKS = {"alone": BLOCKS, "first": BLOCKS, "second": BLOCKS - IN_BLOCKS}
PH, TOPK, KEYS = 8, 16, 128
SLOTS = PH * TOPK
QUARTER = 4
TURNS = SLOTS // QUARTER
LAG = 6
DIAGS = 8
RING = 8
LEVELS = 7
LOWEST = -3.0e38
COUNT0 = 64
HALF = SLOTS // 2
TAB = 1 + 1 + 1 + 1 + LEVELS + H

PAIRS = (NCH - 2) // 2


def uses_of(kind):

    def projection(name, event, m=1, i=0):
        ahead = {"alone": (0,), "first": (0, 1), "second": ()}[kind]
        return [(name + "+" * a, event, m, i, a) for a in ahead]

    def own(*uses):
        return [(*u, 0) for u in uses]

    def level(i):
        steps = {1: own(("retT", "retT", 1, 0)), 2: own(("ret_s", "ret_s", 1, 0)),
                 3: own(("ret_out", "ret_norm", 1, 0), ("ret_kv", "ret_state", 1, 0)),
                 5: projection("gz", "gG_in")}
        return (own((f"P{i}", "inv_P", LEVELS - 1, i - 1)) + steps.get(i, [])
                + own((f"Q{i}", "inv_T", LEVELS - 1, i - 1), (f"R{i}", "inv_TT", LEVELS, i)))

    xT = projection("xT0", "hT", 2, 0), projection("xT1", "hT", 2, 1)
    uses = [u for pair in zip(*xT) for u in pair] + projection("ab", "ab_in")
    for i, name in enumerate(("gq", "gk", "gv")):
        uses += projection(name, f"conv_in{i}")
    uses += own(("gc", "gc_in", 1, 0), ("gc_row", "E", 1, 0), ("beta_row", "kbT", 1, 0))
    uses += projection("rqk", "qk_in") + own(("ssq", "norm_in", 2, 0), ("ssk", "norm_in", 2, 1))
    uses += projection("rv", "vr_in")
    uses += own(("kT", "kst", 1, 0), ("vT", "vb", 1, 0), ("kk", "NT", 1, 0), ("qk", "attn", 1, 0))
    uses += projection("rg", "gR_in") + own(("T1", "inv_TT", LEVELS, 0))
    for i in range(1, LEVELS):
        uses += level(i)
    uses += own(("wT", "wT", 1, 0), ("vnew", "vnew", 1, 0), ("gdn_out", "gdn_norm", 1, 0),
                ("gdn_kv", "gdn_state", 1, 0), ("mT0", "mT", 2, 0), ("mT1", "mT", 2, 1), ("out0", "x2", 2, 0),
                ("out1", "x2", 2, 1), ("h2T0", "h2T", 2, 0), ("h2T1", "h2T", 2, 1))
    for g in range(2):
        uses += own(*[(f"q{i}", "qT", 4, i) for i in (2 * g, 2 * g + 1)])
        uses += own(*[(f"s{i}", "scores", 4, i) for i in (2 * g, 2 * g + 1)])
    return uses


KINDS = ("alone", "first", "second")
USES = {kind: uses_of(kind) for kind in KINDS}
PLACE = {kind: {u[0]: i for i, u in enumerate(USES[kind])} for kind in KINDS}
NUSES = {kind: len(USES[kind]) for kind in KINDS}


class Chunk:

    def __init__(self, n, kind, pair=0):
        self.n, self.kind, self.pair = n, kind, pair
        self.set = int(kind == "second")

    def start(self, per):
        both = per["first"] + per["second"]
        if self.kind == "alone":
            return 0 if self.n == 0 else per["alone"] + PAIRS * both
        return self.pair * both + (per["alone"] + (per["first"] if self.kind == "second" else 0))

    def before(self):
        if self.kind == "second":
            return "first"
        return "alone" if isinstance(self.n, int) and self.n == 1 else "second"


BANKS = 6
FIRST_TURNS = 4
PACE = {
    "alone": "12" "111" "111110" "1" "101010101010" "1111" "11" "1" "1010" "111111000",
    "first": "113" "112" "011110" "1" "111010101010" "1111" "11" "1" "1010" "111111000",
    "second": "1" "121" "11111" "1" "101010101010" "1111" "11" "1" "1110" "111111111",
}



def build(nc, x, w, w_ab, keysT, u_tab, v_tab, cols, rows, head_rows, tables, rope, qdec, small, out):
    with ExitStack() as ctx:
        def sb(name, shape, dt=F32):
            return ctx.enter_context(nc.sbuf_tensor(name, [P, *shape], dt))

        def sem(name):
            return ctx.enter_context(nc.semaphore(name))

        tab = sb("tab", [TAB, P])
        ident, causal, strict, ones = (tab[:, i, :] for i in range(4))
        level_mask = [tab[:, 4 + i, :] for i in range(LEVELS)]
        ret_decay = tab[:, 4 + LEVELS:4 + LEVELS + H, :]
        ropes = sb("ropes", [2, NCH, 32])
        ret_qdec = sb("ret_qdec", [H, P])
        smalls = sb("smalls", [10])
        lnT = sb("lnT", [KT])
        conv_w = sb("conv_w", [12, 4])
        rowsb = sb("rowsb", [2, D])
        ln2_row, lnf_row = rowsb[:, 0, :], rowsb[:, 1, :]
        headsb = sb("headsb", [5 * P + 2 * H])
        retw_row, gdnw_row = headsb[:, 0:512], headsb[:, 512:640]
        a_log, dt_bias = headsb[:, 640:644], headsb[:, 644:648]
        exp_a = sb("exp_a", [H])
        eps_col = sb("eps_col", [1])
        w_ab_sb = sb("w_ab_sb", [KT, 2 * H])
        keys_sb = sb("keys_sb", [16, P])

        wbuf = [sb(f"wbuf{i}", [KT, WB]) for i in range(2)]
        x_in = sb("x_in", [D])
        x2 = sb("x2_row", [D])
        rowbuf = sb("rowbuf", [D])
        actT = sb("actT", [KT, P])
        actT_ahead = sb("actT_ahead", [KT, P])
        x_ahead = actT_ahead[:, :, :].rearrange("p k t -> p (k t)")
        qk_r = [sb(f"qk_r{i}", [2 * H, 2, 32]) for i in range(2)]
        v_r = [sb(f"v_r{i}", [H, DV]) for i in range(2)]
        gate_r = [sb(f"gate_r{i}", [H, DV]) for i in range(2)]
        gate_g = [sb(f"gate_g{i}", [H, DV]) for i in range(2)]
        ab = [sb(f"ab{i}", [2, H]) for i in range(2)]
        conv_in = [sb(f"conv_in{i}", [12, P + 3]) for i in range(2)]
        area = sb("area", [10, 256])
        ret_rot = area[:, 0:2, :].rearrange("p a (h z d) -> p (a h) z d", z=2, d=32)
        ret_tmp = area[:, 2:4, :].rearrange("p a (h z d) -> p (a h) z d", z=2, d=32)
        retT = area[:, 4:6, :].rearrange("p a (b t) -> p (a b) t", t=P)
        ret_qz = area[:, 2:4, :].rearrange("p a (b t) -> p (a b) t", t=P)
        ret_qd = area[:, 0:2, :].rearrange("p a (b t) -> p (a b) t", t=P)
        ret_kd = area[:, 7, :].rearrange("p (h d) -> p h d", d=64)
        ret_s = area[:, 8:10, :].rearrange("p a (b t) -> p (a b) t", t=P)
        flat = area[:, :, :].rearrange("p a b -> p (a b)")
        conv = flat[:, 0:1536].rearrange("p (c t) -> p c t", t=P)
        norms = flat[:, 1536:2560].rearrange("p (c t) -> p c t", t=P)
        cmask = sb("decayT", [H, P])
        expg = sb("expg", [H, P])
        kst = sb("kst", [H, P])
        vnew = area[:, 8:10, :].rearrange("p a (b t) -> p (a b) t", t=P)
        wT = area[:, 6:8, :].rearrange("p a (b t) -> p (a b) t", t=P)
        state_g = sb("state_g", [H, DV])
        state_r = sb("state_r", [2, DV])
        arena = sb("arena", [16, 256])
        half = lambda i: arena[:, 2 * i:2 * i + 2, :].rearrange("p a (b t) -> p (a b) t", t=P)
        NT, attnT, T, TT, Pm, kbe, vb, kbT = (half(i) for i in range(8))
        qdT = kbT
        qT = arena[:, 0:8, :].rearrange("p a (b t) -> p (a b) t", t=P)
        scores = arena[:, 8:16, :].rearrange("p a (b t) -> p (a b) t", t=P)
        cand = qT.rearrange("p (h z) t -> p h (z t)", z=2)
        picked = scores.rearrange("p a (b t) -> p (a b) t", t=TOPK)
        st = sb("st", [64])
        bn = sb("bn", [H, 6])
        mv = sb("mv", [H, 2])
        piece = lambda i, k, dt=F32: area[:, i, 0:k * TOPK].bitcast(dt).rearrange("p (a b) -> p a b", b=TOPK)
        row = lambda i, dt=F32: area[:, i, :].bitcast(dt).rearrange("p (z s) -> p z s", z=2)
        top_v, top_if, best = piece(0, 16), piece(1, 16), piece(2, PH)
        sel, pos_f = row(3), row(4)
        top_i, pos2, pos = piece(5, 16, U32), row(6, U32), row(7, U32)[:, 0, :]
        gate_next = sb("gate_next", [SLOTS])
        ids_next = sb("ids_next", [SLOTS])
        iota_f = sb("iota_f", [TOPK])

        urow = [sb(f"urow{i}", [D]) for i in range(RING)]
        vrow = [sb(f"vrow{i}", [D]) for i in range(RING)]
        h2 = sb("h2", [D])
        ids = sb("ids", [SLOTS], U32)
        gate = sb("gate", [SLOTS])
        dots = sb("dots", [SLOTS])
        gelu = sb("gelu", [SLOTS])
        weight = sb("weight", [SLOTS])
        diag = sb("diag", [DIAGS, P])
        y_sb = diag[:, :, :].rearrange("p k t -> p (k t)")

        bank = [ctx.enter_context(nc.psum_tensor(f"bank{i}", [P, 512], F32)) for i in range(BANKS)]
        y_ps = [ctx.enter_context(nc.psum_tensor(f"y_ps{i}", [P, 512], F32)) for i in range(2)]

        per_chunk = {
            "rms1": 1, "sqrt1": 1, "x_norm": 1, "rot": 1, "ret_qd": 1, "ret_out_ready": 1, "sqrt_ret": 1,
            "ret_mixed": 1, "conv_done": 3, "silu_conv": 3, "sq": 1, "normed": 1, "sp_in": 1, "exp_ab": 1,
            "ln_ab": 1, "beta_g": 1, "diff": 1, "exp_diff": 1, "small_exp": 1, "kst_scale": 1, "qd": 1,
            "kbe": 1, "T_init": 1, "gdn_ss": 1, "gdn_ms": 1, "sqrt_gdn": 1, "mixed": 1, "rms2": 1,
            "sqrt2": 1, "h2": 1, "gate_in": 2, "gate_exp": 2, "routed": 2,
            "peer_in": 1, "peer_in_2": 1, "gelu": PH, "weight": PH, "diag": SLOTS, "yss": 1, "yms": 1,
            "sqrt_y": 1, "y_out": 1, "pe_done": 1,
        }
        for _, e, m, _, _ in USES["alone"]:
            per_chunk[e] = m
        S = {e: sem(e) for e in per_chunk}
        full = sem("bank_full")
        ahead_loaded = sem("ahead_loaded")
        const_in, x_loaded, y_stored = sem("const_in"), sem("x_loaded"), sem("y_stored")
        start_up = sem("start_up")
        passed = sem("passed")
        w_loaded = [sem(f"w_loaded{i}") for i in range(2)]
        w_free = sem("w_free")
        u_loaded = [sem(f"u_loaded{i}") for i in range(RING)]
        v_loaded = [sem(f"v_loaded{i}") for i in range(RING)]
        u_used, v_used = sem("u_used"), sem("v_used")
        mix_chain, peer_chain = sem("mix_chain"), sem("peer_chain")
        late_in = sem("late_in")
        N_CONST, N_LATE = 5, 6

        def event(name, n, i=0):
            return S[name], n * per_chunk[name] + i + 1

        def event_before(name, n):
            return S[name], n * per_chunk[name]

        def used(sem_, n, s):
            return sem_, n * SLOTS + (s + 1 + COUNT0)

        def filled(eng, name, c):
            eng.wait_ge(full, c.start(NUSES) + (PLACE[c.kind][name] + 1))
            return bank[PLACE[c.kind][name] % BANKS]

        def follows(eng, name, n):
            if not isinstance(n, int) or n > 0:
                eng.wait_ge(*event_before(name, n))

        block = ctx.enter_context(nc.Block())

        @block.sync
        def _(sp):
            sp.dma_start(x_in[:, :], x[0]).then_inc(x_loaded, 16)
            for dst, src in ((tab[:, :, :], tables), (lnT[:, :], cols[:, 0:KT]), (w_ab_sb[:, :, :], w_ab),
                             (headsb[:, :], head_rows.partition_broadcast(P)),
                             (conv_w[:, :, :], cols[:, KT:].rearrange("p (c j) -> p c j", j=4))):
                sp.dma_start(dst, src).then_inc(const_in, 16)

            def blocks(c, lo, hi):
                with sp.Fori(0, (hi - lo) // 2) as b:
                    for i in range(2):
                        sp.wait_ge(w_free, c.start(NBLOCKS) + (b * 2 + (i + 1 + lo - skipped(c))))
                        sp.dma_start(wbuf[i][:, :, :], w[bass.ds(b * 2 + (i + lo), 1)].rearrange("o p k c -> (o p) k c")
                                     ).then_inc(w_loaded[i], 16)

            def skipped(c):
                return BLOCKS - NBLOCKS[c.kind]

            def x_rows(n):
                return x[at(n)].rearrange("o p d -> (o p) d")

            def stream(c):
                if c.kind == "first":
                    sp.dma_start(x_ahead, x_rows(c.n + 1)).then_inc(ahead_loaded, 16)
                blocks(c, skipped(c), BLOCKS)

            def next_residual(n):
                sp.wait_ge(*event("x2", n, 1))
                sp.dma_start(x_in[:, :], x_rows(n + 1)).then_inc(x_loaded, 16)

            stream(Chunk(0, "alone"))
            next_residual(0)
            with sp.Fori(0, PAIRS) as p:
                for kind in ("first", "second"):
                    c = Chunk(p * 2 + (1 + (kind == "second")), kind, p)
                    stream(c)
                    next_residual(c.n)
            stream(Chunk(NCH - 1, "alone"))

        @block.gpsimd
        def _(pool):
            nc.gpsimd.iota(ids[:, 0:TOPK], [[1, TOPK]], base=0, channel_multiplier=0).then_inc(start_up, 1)
            pool.wait_ge(start_up, 1)
            nc.gpsimd.tensor_copy(iota_f[:, :], ids[:, 0:TOPK]).then_inc(start_up, 1)

            def gather(table, row, slot, done):
                nc.gpsimd.indirect_dma_start(
                    out=row, out_offset=None, in_=table,
                    in_offset=bass.IndirectOffsetOnAxis(ap=ids[:, slot:slot + 1], axis=0)).then_inc(done, 16)

            with pool.Fori(0, NCH) as n:
                pool.wait_ge(*event("peer_in", n))
                pool.sem_inc(passed, 1)
                for t in range(TURNS + LAG):
                    for q in range(QUARTER):
                        s = QUARTER * t + q
                        if s == HALF:
                            pool.wait_ge(*event("peer_in_2", n))
                            pool.sem_inc(passed, 1)
                        if s < SLOTS:
                            pool.wait_ge(*used(u_used, n, s - RING))
                            pool.sem_inc(passed, 1)
                            gather(u_tab, urow[s % RING][:, :], s, u_loaded[s % RING])
                        s -= QUARTER * LAG
                        if s >= 0:
                            pool.wait_ge(*used(v_used, n, s - RING))
                            pool.sem_inc(passed, 1)
                            gather(v_tab, vrow[s % RING][:, :], s, v_loaded[s % RING])

        @block.tensor
        def _(pe):
            pe.wait_ge(const_in, 16 * N_CONST)
            mm, tr = nc.tensor.matmul, nc.tensor.transpose

            def peer_turn(n, t):
                if t == LAG:
                    pe.wait_ge(*event("x2", n, 1))
                    pe.wait_ge(S["y_out"], n + 1)
                    for j in range(2):
                        mm(y_ps[j][:, :], ident, x2[:, 512 * j:512 * j + 512], start=True, stop=False,
                           skip_group_check=True)
                for s in range(QUARTER * (t - LAG), QUARTER * (t - LAG + 1)):
                    if s < 0 or s >= SLOTS:
                        continue
                    pe.wait_ge(*event("diag", n, s))
                    pe.wait_ge(v_loaded[s % RING], n * (16 * SLOTS // RING) + 16 * (s // RING + 1))
                    for j in range(2):
                        last = mm(y_ps[j][:, :], diag[:, s % DIAGS, :], vrow[s % RING][:, 512 * j:512 * j + 512],
                                  start=False, stop=(s == SLOTS - 1), skip_group_check=True)
                    last.then_inc(v_used, 1)

            def mix(c, turn):
                use, n = [0], c.n
                pairing = c.kind == "first"

                def take(name):
                    u = use[0]
                    assert USES[c.kind][u][0] == name, (USES[c.kind][u], name)
                    use[0] += 1
                    uses, at_n = USES[c.kind], n
                    v = u - BANKS
                    if v < 0 and not first_chunk(n):
                        uses, at_n = USES[c.before()], n - 1
                        v = max(i for i in range(len(uses)) if i % BANKS == u % BANKS)
                    if v >= 0:
                        _, name, _, i, ahead = uses[v]
                        pe.wait_ge(*event(name, at_n + ahead if ahead else at_n, i))
                    return bank[u % BANKS]

                def given(ins):
                    ins.then_inc(full, 1)

                def transposes(name, src, count):
                    b = take(name)
                    for i in range(count):
                        last = tr(b[:, P * i:P * i + P], src(i), ident)
                    given(last)

                blk = [0]

                def weight_block():
                    i = blk[0]
                    blk[0] += 1
                    pe.wait_ge(w_loaded[i % 2], c.start({k: 8 * v for k, v in NBLOCKS.items()}) + 16 * (i // 2 + 1))
                    return wbuf[i % 2]

                def project(name, product, sources):
                    banks = [take(name + "+" * a) for a in range(len(sources))]
                    for half_ in range(2):
                        wb = weight_block()
                        for b, src in zip(banks, sources):
                            last = product(b, half_, wb, src)
                            if half_:
                                given(last)
                        if half_ == 0:
                            last.then_inc(w_free, 1)
                    pe.wait_ge(full, c.start(NUSES) + use[0])
                    pe.sem_inc(w_free, 1)

                def rows_product(b, half_, wb, src):
                    for k in range(KT):
                        last = mm(b[:, WB * half_:WB * half_ + WB], src[:, k, :], wb[:, k, :],
                                  start=(k == 0), stop=(k == KT - 1))
                    return last

                def cols_product(b, half_, wb, src):
                    for i in range(2):
                        o = P * (2 * half_ + i)
                        for k in range(KT):
                            last = mm(b[:, o:o + P], wb[:, k, P * i:P * i + P], src[:, k, :],
                                      start=(k == 0), stop=(k == KT - 1))
                    return last

                projected = [actT, actT_ahead] if pairing else [actT]

                def by_head(name, lhs, rhs):
                    b = take(name)
                    for h in range(H):
                        last = mm(b[:, P * h:P * h + P], lhs[:, h, :], rhs[:, h, :], start=True, stop=True)
                    given(last)

                def all_rows(name, rhs):
                    given(mm(take(name)[:, :], ones, rhs.rearrange("p h t -> p (h t)"), start=True, stop=True))

                turn()
                if c.kind != "second":
                    for a in range(len(projected)):
                        pe.wait_ge(*event("x_norm", n + a if a else n))
                        for j in range(2):
                            transposes(f"xT{j}" + "+" * a,
                                       lambda i: rowbuf[:, P * (4 * j + i):P * (4 * j + i) + P], 4)
                        turn()
                    pe.wait_ge(*event("hT", n + 1 if pairing else n, 1))
                    for a, src in enumerate(projected):
                        b = take("ab" + "+" * a)
                        for k in range(KT):
                            last = mm(b[:, 0:2 * H], src[:, k, :], w_ab_sb[:, k, :], start=(k == 0), stop=(k == KT - 1))
                        given(last)
                for name in ("gq", "gk", "gv"):
                    if c.kind != "second":
                        project(name, cols_product, projected)
                    turn()
                pe.wait_ge(*event("beta_g", n))
                given(mm(take("gc")[:, 0:H], causal, st[:, 20:24], start=True, stop=True))
                all_rows("gc_row", T[:, :, :])
                all_rows("beta_row", TT[:, :, :])
                turn()
                if c.kind != "second":
                    project("rqk", rows_product, projected)
                turn()
                pe.wait_ge(*event("sq", n))
                all_rows("ssq", norms[:, 0:4, :])
                all_rows("ssk", norms[:, 4:8, :])
                turn()
                if c.kind != "second":
                    project("rv", rows_product, projected)
                turn()
                pe.wait_ge(*event("normed", n))
                transposes("kT", lambda i: conv[:, 4 + i, :], 4)
                transposes("vT", lambda i: conv[:, 8 + i, :], 4)
                pe.wait_ge(*event("kbT", n))
                by_head("kk", conv[:, 4:8, :], kbT)
                by_head("qk", conv[:, 4:8, :], conv[:, 0:4, :])
                turn()
                if c.kind != "second":
                    project("rg", rows_product, projected)
                    turn()

                def ret_transposes():
                    pe.wait_ge(*event("rot", n))
                    transposes("retT", lambda i: ret_rot[:, 2 * i:2 * i + 2, :, :].rearrange("p a z d -> p (a z d)"), 4)

                def ret_scores():
                    pe.wait_ge(*event("ret_qd", n))
                    b = take("ret_s")
                    for h in range(H):
                        last = mm(b[:, P * h:P * h + P], retT[:, 2 + h // 2, :], ret_qz[:, h, :], start=True, stop=True)
                    given(last)

                def ret_out():
                    pe.wait_ge(*event("ret_s", n))
                    pe.wait_ge(*event("vr_in", n))
                    follows(pe, "ret_state", n)
                    if isinstance(n, int):
                        pe.wait_ge(start_up, 3)
                    b = take("ret_out")
                    for h in range(H):
                        mm(b[:, P * h:P * h + P], ret_s[:, h, :], v_r[c.set][:, h, :], start=True, stop=False)
                        last = mm(b[:, P * h:P * h + P], ret_qd[:, h, :], state_r[:, h // 2, :], start=False, stop=True)
                    given(last)
                    b = take("ret_kv")
                    for h in range(H):
                        p0 = 64 * (h % 2)
                        last = mm(b[p0:p0 + 64, P * (h // 2):P * (h // 2) + P], ret_kd[:, h, :], v_r[c.set][:, h, :],
                                  start=True, stop=True)
                    given(last)

                def gate_columns():
                    if c.kind != "second":
                        project("gz", rows_product, projected)

                between = {1: ret_transposes, 2: ret_scores, 3: ret_out, 5: gate_columns}

                pe.wait_ge(*event("T_init", n))
                transposes("T1", lambda h: TT[:, h, :], H)
                turn()
                for i in range(1, LEVELS):
                    pe.wait_ge(*event("inv_TT", n, i - 1))
                    by_head(f"P{i}", NT, T)
                    if i in between:
                        between[i]()
                    turn()
                    pe.wait_ge(*event("inv_P", n, i - 1))
                    by_head(f"Q{i}", TT, Pm)
                    by_head(f"R{i}", Pm, TT)
                    turn()
                pe.wait_ge(*event("inv_TT", n, LEVELS - 1))
                pe.wait_ge(*event("kbe", n))
                by_head("wT", kbe, TT)
                turn()
                pe.wait_ge(*event("wT", n))
                follows(pe, "gdn_state", n)
                b = take("vnew")
                for h in range(H):
                    mm(b[:, P * h:P * h + P], TT[:, h, :], vb[:, h, :], start=True, stop=False)
                    last = mm(b[:, P * h:P * h + P], wT[:, h, :], state_g[:, h, :], start=False, stop=True)
                given(last)
                turn()
                pe.wait_ge(*event("vnew", n))
                pe.wait_ge(*event("qd", n))
                b = take("gdn_out")
                for h in range(H):
                    mm(b[:, P * h:P * h + P], qdT[:, h, :], state_g[:, h, :], start=True, stop=False)
                    last = mm(b[:, P * h:P * h + P], attnT[:, h, :], vnew[:, h, :], start=False, stop=True)
                given(last)
                by_head("gdn_kv", kst, vnew)
                turn()
                pe.wait_ge(*event("mixed", n))
                pe.wait_ge(*event("ret_mixed", n))
                for j in range(2):
                    transposes(f"mT{j}", lambda i: rowbuf[:, P * (4 * j + i):P * (4 * j + i) + P], 4)
                turn()
                pe.wait_ge(*event("mT", n, 1))
                for j in range(2):
                    project(f"out{j}", rows_product, [actT])
                    turn()
                pe.wait_ge(*event("h2", n))
                for j in range(2):
                    transposes(f"h2T{j}", lambda i: rowbuf[:, P * (4 * j + i):P * (4 * j + i) + P], 4)
                turn()
                pe.wait_ge(*event("h2T", n, 1))
                if first_chunk(n):
                    pe.wait_ge(late_in, 16 * N_LATE)
                for g in range(2):
                    for j in (2 * g, 2 * g + 1):
                        project(f"q{j}", cols_product, [actT])
                        turn()
                    for j in (2 * g, 2 * g + 1):
                        pe.wait_ge(*event("qT", n, j))
                        b = take(f"s{j}")
                        for i in range(4):
                            last = mm(b[:, P * i:P * i + P], qT[:, 4 * j + i, :], keys_sb[:, 4 * j + i, :],
                                      start=True, stop=True)
                        given(last)
                for _ in range(9):
                    turn()
                assert use[0] == NUSES[c.kind] and blk[0] == NBLOCKS[c.kind]

            pe.sem_inc(w_free, 2)
            pe.sem_inc(v_used, COUNT0)
            chunks(pe, mix, peer_turn, lambda n: None)

        @block.scalar
        def _(act):
            A = nc.scalar.activation

            def peer_turn(n, t):
                if t % QUARTER == 0 and 0 < t <= TURNS:
                    h = t // QUARTER - 1
                    act.wait_ge(*used(u_used, n, TOPK * h + TOPK - 1))
                    A(gelu[:, TOPK * h:TOPK * h + TOPK], dots[:, TOPK * h:TOPK * h + TOPK], ACT.Gelu
                      ).then_inc(S["gelu"], 1)
                for s in range(QUARTER * (t + 1 - LAG), QUARTER * (t + 2 - LAG)):
                    if s < 0 or s >= SLOTS:
                        continue
                    if s % TOPK == 0:
                        act.wait_ge(*event("weight", n, s // TOPK))
                    act.wait_ge(*used(v_used, n, s - DIAGS))
                    A(diag[:, s % DIAGS, :], ident, ACT.Copy, scale=weight[:, s:s + 1]).then_inc(S["diag"], 1)

            def finish(n):
                act.wait_ge(*used(v_used, n, SLOTS - 1))
                A(y_sb[:, 0:512], y_ps[0][:, :], ACT.Square, accum_out=st[:, 60:61])
                A(y_sb[:, 512:1024], y_ps[1][:, :], ACT.Square, accum_out=st[:, 61:62]).then_inc(S["yss"], 1)
                act.wait_ge(*event("yms", n))
                A(st[:, 59:60], st[:, 58:59], ACT.Sqrt).then_inc(S["sqrt_y"], 1)
                act.wait_ge(S["y_out"], n + 2)
                act.dma_start(out[at(n)].rearrange("o p d -> (o p) d"), y_sb[:, :]).then_inc(y_stored, 16)
                act.wait_ge(y_stored, n * 16 + 16)

            def mix(c, turn):
                n = c.n
                ahead = {"alone": (0,), "first": (0, 1), "second": ()}[c.kind]

                def heads(ap):
                    return ap[:, :].rearrange("p (h t) -> p h t", t=P)

                def put(name, use, dst, f=ACT.Copy, **kw):
                    A(dst, heads(filled(act, use, c)), f, **kw).then_inc(S[name], 1)

                def take_in(name, use, sets, f=ACT.Copy):
                    for a in ahead:
                        put(name, use + "+" * a, sets[a], f)

                def conv_silu(j):
                    act.wait_ge(*event("conv_done", n, j))
                    A(conv[:, 4 * j:4 * j + 4, :], conv[:, 4 * j:4 * j + 4, :], ACT.Silu).then_inc(S["silu_conv"], 1)

                turn()
                for a in ahead:
                    act.wait_ge(*event("rms1", n + a if a else n))
                    A(st[:, 1:2], st[:, 0:1], ACT.Sqrt).then_inc(S["sqrt1"], 1)
                    if first_chunk(n):
                        act.wait_ge(const_in, 16 * N_CONST)
                        act.wait_ge(start_up, 3)
                        A(exp_a[:, :], a_log, ACT.Exp).then_inc(start_up, 1)
                        for dst, src in ((ropes[:, :, :, :], rope), (ret_qdec[:, :, :], qdec), (smalls[:, :], small),
                                         (keys_sb[:, :, :], keysT), (ln2_row, rows[0].partition_broadcast(P)),
                                         (lnf_row, rows[1].partition_broadcast(P))):
                            act.dma_start(dst, src).then_inc(late_in, 16)
                    turn()
                act.wait_ge(*event("sp_in", n))
                A(st[:, 8:12], st[:, 4:8], ACT.Exp)
                A(st[:, 12:16], ab[c.set][:, 1, :], ACT.Exp, scale=-1.0).then_inc(S["exp_ab"], 1)
                act.wait_ge(*event("exp_ab", n))
                A(st[:, 16:20], st[:, 8:12], ACT.Ln, bias=1.0).then_inc(S["ln_ab"], 1)
                if ahead:
                    follows(act, "conv_done", n)
                for j, use in enumerate(("gq", "gk", "gv")):
                    take_in(f"conv_in{j}", use, [x_[:, 4 * j:4 * j + 4, 3:P + 3] for x_ in conv_in])
                    if j:
                        conv_silu(j - 1)
                    turn()
                act.wait_ge(*event("diff", n))
                A(cmask[:, :, :], cmask[:, :, :], ACT.Exp)
                A(st[:, 36:44], st[:, 44:52], ACT.Exp).then_inc(S["exp_diff"], 1)
                put("E", "gc_row", expg[:, :, :], ACT.Exp)
                turn()
                conv_silu(2)
                act.wait_ge(*event("silu_conv", n, 1))
                A(norms[:, :, :], conv[:, 0:8, :], ACT.Square).then_inc(S["sq"], 1)
                if ahead:
                    follows(act, "ret_qd", n)
                take_in("qk_in", "rqk", [x_[:, :, :, :].rearrange("p (a h) z d -> p a (h z d)", a=4) for x_ in qk_r])
                turn()
                put("norm_in", "ssq", norms[:, 0:4, :], ACT.Sqrt, bias=eps_col[:, 0:1])
                put("norm_in", "ssk", norms[:, 4:8, :], ACT.Sqrt, bias=eps_col[:, 0:1])
                turn()
                if ahead:
                    follows(act, "ret_state", n)
                take_in("vr_in", "rv", [x_[:, :, :] for x_ in v_r])
                turn()
                turn()
                if ahead:
                    follows(act, "ret_mixed", n)
                    take_in("gR_in", "rg", [x_[:, :, :] for x_ in gate_r], ACT.Silu)
                    turn()
                turn()
                for i in range(1, LEVELS):
                    if i == 5:
                        if ahead:
                            follows(act, "mixed", n)
                        take_in("gG_in", "gz", [x_[:, :, :] for x_ in gate_g], ACT.Silu)
                    if i == 1:
                        put("retT", "retT", retT[:, :, :])
                    turn()
                    if i == 3:
                        act.wait_ge(*event("ret_out_ready", n))
                        A(st[:, 28:32], mv[:, :, 1], ACT.Sqrt, bias=eps_col[:, 0:1]).then_inc(S["sqrt_ret"], 1)
                    turn()
                put("wT", "wT", wT[:, :, :], scale=-1.0)
                turn()
                put("vnew", "vnew", vnew[:, :, :])
                turn()
                b = filled(act, "gdn_out", c)
                for h in range(H):
                    last = A(qdT[:, h, :], b[:, P * h:P * h + P], ACT.Square, accum_out=st[:, 52 + h:53 + h])
                last.then_inc(S["gdn_ss"], 1)
                act.wait_ge(*event("gdn_ms", n))
                A(st[:, 32:36], st[:, 24:28], ACT.Sqrt).then_inc(S["sqrt_gdn"], 1)
                turn()
                for j in range(2):
                    put("mT", f"mT{j}", actT[:, 4 * j:4 * j + 4, :])
                turn()
                turn()
                turn()
                act.wait_ge(*event("rms2", n))
                A(st[:, 1:2], st[:, 0:1], ACT.Sqrt).then_inc(S["sqrt2"], 1)
                for j in range(2):
                    put("h2T", f"h2T{j}", actT[:, 4 * j:4 * j + 4, :])
                turn()
                for g in range(2):
                    for j in (2 * g, 2 * g + 1):
                        put("qT", f"q{j}", qT[:, 4 * j:4 * j + 4, :])
                        turn()
                    for j in (2 * g, 2 * g + 1):
                        put("scores", f"s{j}", scores[:, 4 * j:4 * j + 4, :])
                for g, marks in ((0, 2), (1, 5)):
                    for _ in range(marks):
                        turn()
                    act.wait_ge(*event("gate_in", n, g))
                    A(best[:, 4 * g:4 * g + 4, :], best[:, 4 * g:4 * g + 4, :], ACT.Exp).then_inc(S["gate_exp"], 1)
                for _ in range(2):
                    turn()

            chunks(act, mix, peer_turn, finish)

        @block.vector
        def _(dve):
            V = nc.vector
            MIX_LINKS, PEER_LINKS = {"alone": 71, "first": 74, "second": 68}, 3
            V.memset(state_g[:, :, :], 0.0)
            V.memset(state_r[:, :, :], 0.0)
            V.memset(conv_in[0][:, :, 0:3], 0.0)
            dve.wait_ge(start_up, 2)
            V.memset(eps_col[:, :], EPS).then_inc(start_up, 1)
            dve.wait_ge(start_up, 3)
            dve.sem_inc(u_used, COUNT0)
            dve.sem_inc(S["y_out"], 1)

            def peer_turn(n, t):
                if t == 0:
                    dve.wait_ge(*used(u_used, n, -1))
                    follows(dve, "weight", n)
                    V.tensor_copy(h2[:, :], rowbuf[:, :])
                    V.tensor_copy(gate[:, 0:HALF], gate_next[:, 0:HALF])
                    dve.wait_ge(*used(v_used, n, -HALF - 1))
                    V.tensor_copy(ids[:, 0:HALF], ids_next[:, 0:HALF]).then_inc(S["peer_in"], 1)
                    dve.wait_ge(*event("peer_in", n))
                if t == LAG:
                    V.tensor_copy(gate[:, HALF:], gate_next[:, HALF:])
                    dve.wait_ge(*used(v_used, n, -1))
                    V.tensor_copy(ids[:, HALF:], ids_next[:, HALF:]).then_inc(S["peer_in_2"], 1)
                    dve.wait_ge(*event("peer_in_2", n))
                if t < TURNS:
                    for s in range(QUARTER * t, QUARTER * t + QUARTER):
                        u = urow[s % RING][:, :]
                        dve.wait_ge(u_loaded[s % RING], n * (16 * SLOTS // RING) + 16 * (s // RING + 1))
                        V.tensor_tensor_reduce(out=u, in0=u, in1=h2[:, :], scale=1.0, scalar=0.0, op0=ALU.mult,
                                               op1=ALU.add, accum_out=dots[:, s:s + 1]).then_inc(u_used, 1)
                if t % QUARTER == 0 and 0 < t <= TURNS:
                    h = t // QUARTER - 1
                    c0, c1 = TOPK * h, TOPK * h + TOPK
                    dve.wait_ge(*event("gelu", n, h))
                    V.tensor_tensor(weight[:, c0:c1], gelu[:, c0:c1], gate[:, c0:c1], ALU.mult).then_inc(S["weight"], 1)

            def finish(n):
                base = n * PEER_LINKS
                dve.wait_ge(*event("yss", n))
                V.tensor_tensor(st[:, 57:58], st[:, 60:61], st[:, 61:62], ALU.add).then_inc(peer_chain, 1)
                dve.wait_ge(peer_chain, base + 1)
                V.tensor_scalar(st[:, 58:59], st[:, 57:58], 1.0 / D, EPS, ALU.mult, ALU.add).then_inc(S["yms"], 1)
                dve.wait_ge(*event("sqrt_y", n))
                V.reciprocal(st[:, 57:58], st[:, 59:60]).then_inc(peer_chain, 1)
                dve.wait_ge(peer_chain, base + 2)
                V.scalar_tensor_tensor(y_sb[:, 0:512], y_ps[0][:, :], st[:, 57:58], lnf_row[:, 0:512],
                                       ALU.mult, ALU.mult).then_inc(peer_chain, 1)
                V.scalar_tensor_tensor(y_sb[:, 512:1024], y_ps[1][:, :], st[:, 57:58], lnf_row[:, 512:1024],
                                       ALU.mult, ALU.mult).then_inc(S["y_out"], 1)

            def mix(c, turn):
                links, n = [0], c.n
                ahead = {"alone": (0,), "first": (0, 1), "second": ()}[c.kind]

                def link(ins, apart=False):
                    links[0] += 1
                    ins.then_inc(mix_chain, 1)
                    dve.wait_ge(mix_chain, c.start(MIX_LINKS) + links[0])
                    if apart:
                        dve.sem_inc(passed, 1)

                def heads(ap):
                    return ap[:, :].rearrange("p (h t) -> p h t", t=P)

                def by_head(ap, k=P):
                    return ap.unsqueeze(2).broadcast_to([P, ap.shape[1], k])

                def each_head(ap):
                    return ap.unsqueeze(1).broadcast_to([P, H, P])

                turn()
                for a in ahead:
                    m = n + a if a else n
                    rows_in = x_ahead if a else x_in[:, :]
                    if a:
                        dve.wait_ge(ahead_loaded, c.pair * 16 + 16)
                    else:
                        dve.wait_ge(x_loaded, n * 16 + 16)
                    link(V.tensor_tensor_reduce(out=rowbuf[:, :], in0=rows_in, in1=rows_in, scale=1.0, scalar=0.0,
                                                op0=ALU.mult, op1=ALU.add, accum_out=st[:, 2:3]))
                    V.tensor_scalar(st[:, 0:1], st[:, 2:3], 1.0 / D, EPS, ALU.mult, ALU.add).then_inc(S["rms1"], 1)
                    dve.wait_ge(*event("sqrt1", m))
                    link(V.reciprocal(st[:, 2:3], st[:, 1:2]))
                    V.tensor_scalar(rowbuf[:, :], rows_in, st[:, 2:3], None, ALU.mult).then_inc(S["x_norm"], 1)
                    turn()
                    if first_chunk(n):
                        dve.wait_ge(const_in, 16 * N_CONST)
                    for j in range(2):
                        V.tensor_tensor((actT_ahead if a else actT)[:, 4 * j:4 * j + 4, :],
                                        heads(filled(dve, f"xT{j}" + "+" * a, c)),
                                        by_head(lnT[:, 4 * j:4 * j + 4]), ALU.mult).then_inc(S["hT"], 1)
                for a in ahead:
                    link(V.tensor_copy(ab[a][:, :, :].rearrange("p a h -> p (a h)"),
                                       filled(dve, "ab" + "+" * a, c)[:, 0:2 * H]))
                    V.tensor_copy(st[:, 3:4], ab[a][:, 0, 0:1]).then_inc(S["ab_in"], 1)
                link(V.tensor_tensor(st[:, 52:56], ab[c.set][:, 0, :], dt_bias, ALU.add))
                link(V.tensor_scalar(st[:, 4:8], st[:, 52:56], -1.0, None, ALU.mult))
                V.tensor_tensor(st[:, 4:8], st[:, 4:8], st[:, 52:56], ALU.min).then_inc(S["sp_in"], 1)

                def convolve(part):
                    dve.wait_ge(*event(f"conv_in{part}", n))
                    for j in range(4):
                        for i in range(4 * part, 4 * part + 4):
                            src, dst = conv_in[c.set][:, i, j:j + P], conv[:, i, :]
                            if j == 0:
                                last = V.tensor_scalar(dst, src, conv_w[:, i, 0:1], None, ALU.mult)
                            else:
                                last = V.scalar_tensor_tensor(dst, src, conv_w[:, i, j:j + 1], dst, ALU.mult, ALU.add)
                        link(last)
                    here, there = conv_in[c.set], conv_in[int(c.kind == "first")]
                    V.tensor_copy(there[:, 4 * part:4 * part + 4, 0:3], here[:, 4 * part:4 * part + 4, P:P + 3]
                                  ).then_inc(S["conv_done"], 1)

                convolve(0)
                turn()
                if first_chunk(n):
                    dve.wait_ge(start_up, 4)
                dve.wait_ge(*event("ln_ab", n))
                link(V.tensor_scalar(st[:, 4:8], st[:, 52:56], 0.0, None, ALU.max))
                V.tensor_scalar(st[:, 12:16], st[:, 12:16], 1.0, None, ALU.add)
                link(V.tensor_tensor(st[:, 4:8], st[:, 4:8], st[:, 16:20], ALU.add))
                V.scalar_tensor_tensor(st[:, 20:24], st[:, 4:8], -1.0, exp_a[:, :], ALU.mult, ALU.mult)
                link(V.reciprocal(st[:, 24:28], st[:, 12:16]))
                V.tensor_tensor(T[:, :, :], each_head(causal), by_head(st[:, 20:24]), ALU.mult)
                V.tensor_tensor(TT[:, :, :], each_head(ident), by_head(st[:, 24:28]), ALU.mult).then_inc(S["beta_g"], 1)
                convolve(1)
                turn()
                convolve(2)
                turn()
                link(V.tensor_copy(st[:, 44:48], filled(dve, "gc", c)[:, 0:H]))
                V.tensor_copy(st[:, 3:4], st[:, 44:45]).then_inc(S["gc_in"], 1)
                b = filled(dve, "gc_row", c)
                for h in range(H):
                    V.tensor_scalar(cmask[:, h, :], b[:, P * h:P * h + P], st[:, 44 + h:45 + h], 0.0,
                                    ALU.subtract, ALU.min)
                V.tensor_tensor(st[:, 48:52], heads(b)[:, :, P - 1], st[:, 44:48], ALU.subtract).then_inc(S["diff"], 1)
                turn()
                dve.wait_ge(*event("exp_diff", n))
                V.tensor_tensor(st[:, 36:40], st[:, 36:40], st[:, 24:28], ALU.mult)
                link(V.tensor_tensor(cmask[:, :, :], cmask[:, :, :], each_head(causal), ALU.mult))
                turn()
                turn()
                dve.wait_ge(*event("norm_in", n, 1))
                link(V.reciprocal(norms[:, :, :], norms[:, :, :]))
                V.scalar_tensor_tensor(conv[:, 0:4, :].rearrange("p h t -> p (h t)"),
                                       conv[:, 0:4, :].rearrange("p h t -> p (h t)"), float(DV) ** -0.5,
                                       norms[:, 0:4, :].rearrange("p h t -> p (h t)"), ALU.mult, ALU.mult)
                V.tensor_tensor(conv[:, 4:8, :], conv[:, 4:8, :], norms[:, 4:8, :], ALU.mult).then_inc(S["normed"], 1)
                dve.wait_ge(*event("normed", n))
                V.tensor_tensor(kbT[:, :, :], conv[:, 4:8, :], heads(filled(dve, "beta_row", c)), ALU.mult
                                ).then_inc(S["kbT"], 1)
                turn()
                b = filled(dve, "kT", c)
                V.tensor_tensor(kbe[:, :, :], heads(b), by_head(st[:, 36:40]), ALU.mult).then_inc(S["kbe"], 1)
                V.tensor_tensor(kst[:, :, :], heads(b), by_head(st[:, 40:44]), ALU.mult).then_inc(S["kst"], 1)
                V.tensor_tensor(vb[:, :, :], heads(filled(dve, "vT", c)), by_head(st[:, 24:28]), ALU.mult
                                ).then_inc(S["vb"], 1)
                link(V.tensor_tensor(NT[:, :, :], heads(filled(dve, "kk", c)), cmask[:, :, :], ALU.mult))
                V.tensor_tensor(NT[:, :, :], NT[:, :, :], each_head(strict), ALU.mult).then_inc(S["NT"], 1)
                dve.wait_ge(*event("NT", n))
                link(V.tensor_tensor(TT[:, :, :], NT[:, :, :], each_head(level_mask[0]), ALU.mult))
                V.tensor_tensor(TT[:, :, :], each_head(ident), TT[:, :, :], ALU.subtract).then_inc(S["T_init"], 1)
                V.tensor_tensor(attnT[:, :, :], heads(filled(dve, "qk", c)), cmask[:, :, :], ALU.mult
                                ).then_inc(S["attn"], 1)
                dve.wait_ge(*event("E", n))
                V.tensor_tensor(qdT[:, :, :], conv[:, 0:4, :], expg[:, :, :], ALU.mult).then_inc(S["qd"], 1)
                dve.wait_ge(*event("qd", n))
                turn()
                if first_chunk(n):
                    dve.wait_ge(late_in, 16 * N_LATE)
                dve.wait_ge(*event("qk_in", n))
                q1, q2 = qk_r[c.set][:, :, 0, :], qk_r[c.set][:, :, 1, :]
                cos, sin = (ropes[:, i, at(n), :].broadcast_to([P, 2 * H, 32]) for i in range(2))
                V.tensor_tensor(ret_rot[:, :, 0, :], q1, cos, ALU.mult)
                V.tensor_tensor(ret_rot[:, :, 1, :], q2, cos, ALU.mult)
                V.tensor_tensor(ret_tmp[:, :, 0, :], q2, sin, ALU.mult)
                link(V.tensor_tensor(ret_tmp[:, :, 1, :], q1, sin, ALU.mult))
                V.tensor_tensor(ret_rot[:, :, 0, :], ret_rot[:, :, 0, :], ret_tmp[:, :, 0, :], ALU.subtract)
                V.tensor_tensor(ret_rot[:, :, 1, :], ret_rot[:, :, 1, :], ret_tmp[:, :, 1, :], ALU.add
                                ).then_inc(S["rot"], 1)
                dve.wait_ge(*event("rot", n))
                V.tensor_tensor(ret_kd[:, :, :], ret_rot[:, H:2 * H, :, :].rearrange("p h z d -> p h (z d)"),
                                by_head(smalls[:, 0:4], 64), ALU.mult)
                if ahead:
                    turn()

                def ret_queries():
                    dve.wait_ge(*event("retT", n))
                    for h in range(H):
                        V.tensor_scalar(ret_qz[:, h, :], retT[:, h // 2, :], smalls[:, 6 + h:7 + h], None, ALU.mult)
                        last = V.tensor_tensor(ret_qd[:, h, :], retT[:, h // 2, :], ret_qdec[:, h, :], ALU.mult)
                    last.then_inc(S["ret_qd"], 1)

                def ret_decay_scores():
                    V.tensor_tensor(ret_s[:, :, :], heads(filled(dve, "ret_s", c)), ret_decay, ALU.mult
                                    ).then_inc(S["ret_s"], 1)

                def ret_moments():
                    b = filled(dve, "ret_kv", c)
                    for j in range(2):
                        last = V.scalar_tensor_tensor(state_r[:, j, :], state_r[:, j, :], smalls[:, 4 + j:5 + j],
                                                      b[:, P * j:P * j + P], ALU.mult, ALU.add)
                    last.then_inc(S["ret_state"], 1)
                    b = filled(dve, "ret_out", c)
                    for h in range(H):
                        last = V.bn_stats(bn[:, h, :], b[:, P * h:P * h + P])
                    link(last, apart=True)
                    for h in range(H):
                        last = V.bn_aggr(mv[:, h, :], bn[:, h, :])
                    last.then_inc(S["ret_out_ready"], 1)
                    dve.wait_ge(*event("gR_in", n))
                    gate_rows = gate_r[c.set][:, :, :].rearrange("p h d -> p (h d)")
                    V.tensor_tensor(gate_rows, gate_rows, retw_row, ALU.mult)

                def ret_group_norm():
                    dve.wait_ge(*event("sqrt_ret", n))
                    b = filled(dve, "ret_out", c)
                    link(V.reciprocal(st[:, 32:36], st[:, 28:32]))
                    for h in range(H):
                        last = V.tensor_scalar(ret_s[:, h, :], b[:, P * h:P * h + P], mv[:, h, 0:1],
                                               st[:, 32 + h:33 + h], ALU.subtract, ALU.mult)
                    last.then_inc(S["ret_norm"], 1)
                    dve.wait_ge(*event("ret_norm", n))
                    V.tensor_tensor(rowbuf[:, 0:512], ret_s[:, :, :].rearrange("p h d -> p (h d)"),
                                    gate_r[c.set][:, :, :].rearrange("p h d -> p (h d)"), ALU.mult
                                    ).then_inc(S["ret_mixed"], 1)

                def gate_weight():
                    dve.wait_ge(*event("gG_in", n))
                    V.tensor_tensor(gate_g[c.set][:, :, :], gate_g[c.set][:, :, :], each_head(gdnw_row), ALU.mult)

                between = {1: ret_queries, 2: ret_decay_scores, 3: ret_moments, 4: ret_group_norm, 5: gate_weight}
                V.tensor_copy(T[:, :, :], heads(filled(dve, "T1", c))).then_inc(S["inv_TT"], 1)
                turn()
                for i in range(1, LEVELS):
                    V.tensor_tensor(Pm[:, :, :], heads(filled(dve, f"P{i}", c)), each_head(level_mask[i]), ALU.mult
                                    ).then_inc(S["inv_P"], 1)
                    if i in between:
                        between[i]()
                    turn()
                    b2 = filled(dve, f"R{i}", c)
                    b = bank[PLACE[c.kind][f"Q{i}"] % BANKS]
                    V.tensor_tensor(T[:, :, :], T[:, :, :], heads(b), ALU.subtract).then_inc(S["inv_T"], 1)
                    V.tensor_tensor(TT[:, :, :], TT[:, :, :], heads(b2), ALU.subtract).then_inc(S["inv_TT"], 1)
                    turn()
                turn()
                turn()
                b = filled(dve, "gdn_out", c)
                dve.wait_ge(*event("gdn_ss", n))
                V.tensor_scalar(st[:, 24:28], st[:, 52:56], 1.0 / DV, EPS, ALU.mult, ALU.add).then_inc(S["gdn_ms"], 1)
                b2 = filled(dve, "gdn_kv", c)
                for h in range(H):
                    last = V.scalar_tensor_tensor(state_g[:, h, :], state_g[:, h, :], expg[:, h, P - 1:P],
                                                  b2[:, P * h:P * h + P], ALU.mult, ALU.add)
                last.then_inc(S["gdn_state"], 1)
                dve.wait_ge(*event("sqrt_gdn", n))
                link(V.reciprocal(st[:, 28:32], st[:, 32:36]))
                for h in range(H):
                    last = V.scalar_tensor_tensor(rowbuf[:, 512 + P * h:512 + P * h + P], b[:, P * h:P * h + P],
                                                  st[:, 28 + h:29 + h], gate_g[c.set][:, h, :], ALU.mult, ALU.mult)
                last.then_inc(S["gdn_norm"], 1)
                V.tensor_copy(st[:, 3:4], st[:, 28:29]).then_inc(S["mixed"], 1)
                turn()
                turn()
                for j in range(2):
                    b = filled(dve, f"out{j}", c)
                    if j == 0 and (not isinstance(n, int) or n > 0):
                        dve.wait_ge(*used(v_used, n - 1, 0))
                    V.tensor_tensor(x2[:, 512 * j:512 * j + 512], b[:, :], x_in[:, 512 * j:512 * j + 512], ALU.add
                                    ).then_inc(S["x2"], 1)
                    turn()
                dve.wait_ge(*event("x2", n, 1))
                link(V.tensor_tensor_reduce(out=rowbuf[:, :], in0=x2[:, :], in1=x2[:, :], scale=1.0, scalar=0.0,
                                            op0=ALU.mult, op1=ALU.add, accum_out=st[:, 2:3]))
                V.tensor_scalar(st[:, 0:1], st[:, 2:3], 1.0 / D, EPS, ALU.mult, ALU.add).then_inc(S["rms2"], 1)
                dve.wait_ge(*event("sqrt2", n))
                link(V.reciprocal(st[:, 2:3], st[:, 1:2]))
                V.scalar_tensor_tensor(rowbuf[:, :], x2[:, :], st[:, 2:3], ln2_row, ALU.mult, ALU.mult
                                       ).then_inc(S["h2"], 1)
                turn()
                turn()
                turn()

                def top16(tiles, src, vals, index):
                    for o in (0, 8):
                        for t in tiles:
                            last = V.max(vals(t)[:, o:o + 8], src(t))
                        link(last, apart=True)
                        for t in tiles:
                            last = V.max_index(index(t)[:, o:o + 8], vals(t)[:, o:o + 8], src(t))
                        if o == 0:
                            for t in tiles:
                                last = V.match_replace(src(t), vals(t)[:, 0:8], src(t), LOWEST)
                        link(last, apart=True)
                        turn()

                iota_all = iota_f[:, :].unsqueeze(1).broadcast_to([P, HALF, TOPK])
                for g in range(2):
                    dve.wait_ge(*event("scores", n, 2 * g + 1))
                    dve.sem_inc(passed, 1)
                    some, halves, mine = range(4 * g, 4 * g + 4), slice(8 * g, 8 * g + 8), slice(HALF * g, HALF * g + HALF)
                    top16(range(8 * g, 8 * g + 8), lambda t: scores[:, t, :], lambda t: top_v[:, t, :],
                          lambda t: top_i[:, t, :])
                    V.tensor_copy(top_if[:, halves, :], top_i[:, halves, :])
                    for h in some:
                        last = V.tensor_tensor(
                            cand[:, h, :].rearrange("p (a b) -> p a b", b=TOPK),
                            top_v[:, 2 * h, :].unsqueeze(2).broadcast_to([P, TOPK, TOPK]),
                            top_v[:, 2 * h + 1, :].unsqueeze(1).broadcast_to([P, TOPK, TOPK]), ALU.add)
                    link(last, apart=True)
                    top16(some, lambda t: cand[:, t, :], lambda t: best[:, t, :],
                          lambda t: pos[:, TOPK * t:TOPK * t + TOPK])
                    heads4 = slice(4 * g, 4 * g + 4)
                    link(V.tensor_copy(st[:, 52:56], best[:, heads4, 0]))
                    V.tensor_tensor(best[:, heads4, :], best[:, heads4, :], by_head(st[:, 52:56], TOPK), ALU.subtract
                                    ).then_inc(S["gate_in"], 1)
                    V.tensor_scalar(pos2[:, 0, mine], pos[:, mine], 4, None, ALU.logical_shift_right)
                    link(V.tensor_scalar(pos2[:, 1, mine], pos[:, mine], TOPK - 1, None, ALU.bitwise_and))
                    link(V.tensor_copy(pos_f[:, :, mine], pos2[:, :, mine]))
                    for z in range(2):
                        pk = picked[:, mine, :]
                        link(V.tensor_tensor(pk, by_head(pos_f[:, z, mine], TOPK), iota_all, ALU.is_equal))
                        for h in some:
                            one_head = picked[:, TOPK * h:TOPK * h + TOPK, :]
                            last = V.tensor_tensor(one_head, one_head, top_if[:, 2 * h + z, :].unsqueeze(1)
                                                   .broadcast_to([P, TOPK, TOPK]), ALU.mult)
                        link(last)
                        link(V.tensor_reduce(sel[:, z, mine], pk, AX, ALU.add))
                        if z == 0:
                            turn()
                    V.scalar_tensor_tensor(ids_next[:, mine], sel[:, 0, mine], float(KEYS), sel[:, 1, mine],
                                           ALU.mult, ALU.add)
                    dve.wait_ge(*event("gate_exp", n, g))
                    link(V.tensor_reduce(st[:, 52:56], best[:, heads4, :], AX, ALU.add))
                    link(V.reciprocal(st[:, 52:56], st[:, 52:56]))
                    V.tensor_tensor(gate_next[:, mine].rearrange("p (h k) -> p h k", k=TOPK), best[:, heads4, :],
                                    by_head(st[:, 52:56], TOPK), ALU.mult).then_inc(S["routed"], 1)
                    dve.wait_ge(*event("routed", n, g))
                turn()
                assert links[0] == MIX_LINKS[c.kind], (c.kind, links)

            chunks(dve, mix, peer_turn, finish)


def first_chunk(n):
    return isinstance(n, int) and n == 0


def at(n):
    return slice(n, n + 1) if isinstance(n, int) else bass.ds(n, 1)


def chunks(eng, mix, peer_turn, finish):
    def together(n, mixed=None, from_turn=0, first=False):
        t, mark = [from_turn], [0]

        def turn():
            mark[0] += 1
            for _ in range(int(PACE[mixed.kind][mark[0] - 1])):
                one()

        def one():
            if t[0] < TURNS + LAG:
                if t[0] == LAG - 1 and not first:
                    finish(n - 1)
                peer_turn(n, t[0])
                t[0] += 1

        if mixed is not None:
            mix(mixed, turn)
            assert mark[0] == len(PACE[mixed.kind]), (mixed.kind, mark)
        while t[0] < TURNS + LAG:
            one()

    early, mark = [0], [0]

    def first_turns():
        mark[0] += 1
        if len(PACE["alone"]) - 6 < mark[0] <= len(PACE["alone"]) - 6 + FIRST_TURNS:
            peer_turn(0, early[0])
            early[0] += 1

    def pair(p, first=False):
        n = 2 * p if isinstance(p, int) else p * 2
        together(n, Chunk(n + 1, "first", p), FIRST_TURNS * first, first)
        together(n + 1, Chunk(n + 2, "second", p))

    mix(Chunk(0, "alone"), first_turns)
    pair(0, first=True)
    with eng.Fori(1, PAIRS) as p:
        pair(p)
    together(NCH - 2, Chunk(NCH - 1, "alone"))
    together(NCH - 1)
    finish(NCH - 1)


def shape_tables():
    i = np.arange(P)
    tables = np.zeros((P, TAB, P), np.float32)
    tables[:, 0] = np.eye(P)
    tables[:, 1] = i[:, None] <= i[None, :]
    tables[:, 2] = i[:, None] < i[None, :]
    tables[:, 3] = 1.0
    for l in range(LEVELS):
        r, c = i[:, None] >> l, i[None, :] >> l
        join = (r % 2 == 1) & (c == r - 1)
        tables[:, 4 + l] = join.T if l == 0 else join
    lg = np.log1p(-np.exp2(-5.0 - np.arange(H)))
    diff = (i[None, :] - i[:, None]).astype(np.float64)
    for h in range(H):
        tables[:, 4 + LEVELS + h] = np.where(diff >= 0, np.exp(lg[h] * np.maximum(diff, 0)), 0) * 64 ** -0.5
    inv = np.float32(10000.0) ** (-np.arange(32, dtype=np.float32) / np.float32(32))
    ang = (np.arange(SEQ, dtype=np.float32)[:, None] * inv[None, :].astype(np.float32)).reshape(NCH, P, 32)
    ang = ang.transpose(1, 0, 2).astype(np.float64)
    rope = np.stack([np.cos(ang), np.sin(ang)], 1).astype(np.float32)
    of = np.array([[2 * j + p // 64 for j in range(2)] for p in range(P)])
    here = (np.arange(H)[None, :] % 2 == i[:, None] // 64).astype(np.float64)
    qdec = (np.exp(lg[:, None] * (i + 1.0)[None, :])[None] * here[:, :, None]).astype(np.float32)
    small = np.concatenate([np.exp(lg[None, :] * (P - 1.0 - i)[:, None]) * 64 ** -0.5, np.exp(lg[of] * P), here], 1)
    return tables, rope, qdec, np.ascontiguousarray(small, np.float32)


def kernel(**inputs):
    import concourse.bacc as bacc
    from concourse.bass_utils import run_bass_kernel_spmd

    a = {k: np.asarray(v) for k, v in inputs.items()}

    def tiles(m, block):
        return m.reshape(KT, P, -1, block).transpose(2, 1, 0, 3)

    w_in = a["w_in"][0]
    by_use = np.r_[6:12, 0:6, 12:14]
    w = np.concatenate([tiles(w_in[:, 0:IN_BLOCKS * WB], WB)[by_use], tiles(a["w_out"][0], WB), tiles(a["peer_wq"][0], WB)])
    w_ab = tiles(w_in[:, IN_BLOCKS * WB:], 2 * H)[0]
    cols = np.concatenate([a["ln1_w"][0].reshape(KT, P).T,
                           a["conv_w"][0].reshape(4, 12, P).transpose(2, 1, 0).reshape(P, 48)], 1)
    head_rows = np.concatenate([a["ret_norm_w"][0], a["gdn_norm_w"][0], a["A_log"][0], a["dt_bias"][0]])
    tables, rope, qdec, small = shape_tables()
    arrays = {
        "x": a["x"].reshape(NCH, P, D), "w": w, "w_ab": w_ab,
        "keysT": a["peer_keys"][0].reshape(16, KEYS, P).transpose(2, 0, 1),
        "u_tab": a["peer_u"][0], "v_tab": a["peer_v"][0], "cols": cols,
        "rows": np.stack([a["ln2_w"][0], a["lnf_w"]]), "head_rows": head_rows,
        "tables": tables, "rope": rope, "qdec": qdec, "small": small,
    }
    nc = bacc.Bacc("TRN2", target_bir_lowering=False, num_devices=1)
    arrays = {k: np.ascontiguousarray(v) for k, v in arrays.items()}
    args = [nc.dram_tensor(k, v.shape, mybir.dt.from_np(v.dtype), kind="ExternalInput").ap() for k, v in arrays.items()]
    args.append(nc.dram_tensor("y", (NCH, P, D), F32, kind="ExternalOutput").ap())
    build(nc, *args)
    r = run_bass_kernel_spmd(nc, [arrays], core_ids=[0])
    return r.results[0]["y"].reshape(1, SEQ, D)
```
